# Optimizing a Trainium2 kernel written in Bass

```python
import jax
import jax.numpy as jnp
from jax import lax
import numpy as np

D_MODEL = 1024
BATCH = 1
SEQ = 1024
DEPTH = 1

CHUNK = 64
NORM_EPS = 1e-6
MIX_WIDTH = D_MODEL
POOL_WIDTH = MIX_WIDTH // 2
POOL_WINDOWS = (2, 4, 8, 16)
POOL_GROUPS = len(POOL_WINDOWS)
POOL_GROUP_DIM = POOL_WIDTH // POOL_GROUPS
GDN_HEAD_DIM = 128
GDN_WIDTH = MIX_WIDTH - POOL_WIDTH
GDN_HEADS = GDN_WIDTH // GDN_HEAD_DIM
CONV_WIDTH = 4
SPLIT_POINTS = (POOL_WIDTH, POOL_WIDTH + GDN_WIDTH, POOL_WIDTH + 2 * GDN_WIDTH, POOL_WIDTH + 3 * GDN_WIDTH, POOL_WIDTH + 4 * GDN_WIDTH, POOL_WIDTH + 4 * GDN_WIDTH + GDN_HEADS)
IN_PROJ_COLS = POOL_WIDTH + 4 * GDN_WIDTH + 2 * GDN_HEADS
PEER_HEADS = 8
PEER_N_KEYS = 128
PEER_N_EXPERTS = PEER_N_KEYS * PEER_N_KEYS
PEER_QUERY_DIM = 256
PEER_HALF = PEER_QUERY_DIM // 2
PEER_TOPK = 16
PEER_TOKEN_BLOCK = 128

kernel_name = "hybrid_pool_gdn_peer_block"

def rms_norm(x, gain):
    xf = x.astype(jnp.float32)
    y = xf * lax.rsqrt(jnp.mean(xf * xf, axis=-1, keepdims=True) + NORM_EPS)
    return (y * gain.astype(jnp.float32)).astype(x.dtype)

def l2_normalize(x):
    return x * lax.rsqrt(jnp.sum(x * x, axis=-1, keepdims=True) + NORM_EPS)

def multiscale_pool_mixer(xp, w_pool, b_pool, pool_scale):
    B, S, _ = xp.shape
    xg = xp.astype(jnp.float32).reshape(B, S, POOL_GROUPS, POOL_GROUP_DIM)
    cs = jnp.cumsum(xg, axis=1)
    pos = jnp.arange(S)
    outs = []
    for gi, win in enumerate(POOL_WINDOWS):
        c = cs[:, :, gi]
        prev = jnp.pad(c, ((0, 0), (win, 0), (0, 0)))[:, :S]
        count = jnp.minimum(pos + 1, win).astype(jnp.float32)[None, :, None]
        outs.append((c - prev) / count - xg[:, :, gi])
    d = jnp.stack(outs, axis=2)
    y = jnp.einsum('bsgc,gcd->bsgd', d, w_pool.astype(jnp.float32)) + b_pool.astype(jnp.float32)
    return (y.reshape(B, S, POOL_WIDTH) * pool_scale.astype(jnp.float32)).astype(xp.dtype)

def causal_depthwise_conv(x, w):
    C = x.shape[-1]
    return lax.conv_general_dilated(
        x, w[:, None, :].astype(x.dtype), window_strides=(1,),
        padding=((CONV_WIDTH - 1, 0),), dimension_numbers=('NWC', 'WIO', 'NWC'),
        feature_group_count=C)

def gated_delta_rule_chunked(q, k, v, g, beta):
    B, S, H, Dk = q.shape
    Dv = v.shape[-1]
    N = S // CHUNK

    def to_chunks(t):
        return t.reshape((B, N, CHUNK) + t.shape[2:]).swapaxes(2, 3)

    qc, kc, vc, gc, bc = (to_chunks(t) for t in (q, k, v, g, beta))
    gcum = jnp.cumsum(gc, axis=-1)
    idx = jnp.arange(CHUNK)
    causal = idx[:, None] >= idx[None, :]
    strict = idx[:, None] > idx[None, :]
    diff = gcum[..., :, None] - gcum[..., None, :]
    decay = jnp.where(causal, jnp.exp(jnp.where(causal, diff, 0.0)), 0.0)
    k_beta = kc * bc[..., None]
    v_beta = vc * bc[..., None]
    kk = jnp.einsum('bnhid,bnhjd->bnhij', k_beta, kc)
    a_mat = jnp.where(strict, kk * decay, 0.0) + jnp.eye(CHUNK, dtype=jnp.float32)
    rhs = jnp.concatenate([v_beta, k_beta * jnp.exp(gcum)[..., None]], axis=-1)
    sol = lax.linalg.triangular_solve(a_mat, rhs, left_side=True, lower=True, unit_diagonal=True)
    u = sol[..., :Dv]
    w = sol[..., Dv:]
    qk = jnp.einsum('bnhid,bnhjd->bnhij', qc, kc) * decay
    q_dec = qc * jnp.exp(gcum)[..., None]
    k_dec = kc * jnp.exp(gcum[..., -1:] - gcum)[..., None]
    chunk_decay = jnp.exp(gcum[..., -1])

    def step(state, inp):
        qk_n, qd_n, kd_n, u_n, w_n, cd_n = inp
        v_new = u_n - jnp.einsum('bhcd,bhde->bhce', w_n, state)
        o_n = jnp.einsum('bhcd,bhde->bhce', qd_n, state) + jnp.einsum('bhij,bhje->bhie', qk_n, v_new)
        state = state * cd_n[..., None, None] + jnp.einsum('bhcd,bhce->bhde', kd_n, v_new)
        return state, o_n

    xs = tuple(jnp.moveaxis(t, 1, 0) for t in (qk, q_dec, k_dec, u, w, chunk_decay))
    state0 = jnp.zeros((B, H, Dk, Dv), jnp.float32)
    _, o = lax.scan(step, state0, xs)
    return jnp.moveaxis(o, 0, 1).swapaxes(2, 3).reshape(B, S, H, Dv)

def gated_deltanet_mixer(q_raw, k_raw, v_raw, z, b_raw, a_raw, conv_w, a_log, dt_bias, o_gain):
    B, S, _ = q_raw.shape
    qkv = jnp.concatenate([q_raw, k_raw, v_raw], axis=-1)
    qkv = jax.nn.silu(causal_depthwise_conv(qkv, conv_w).astype(jnp.float32))
    q, k, v = jnp.split(qkv, 3, axis=-1)
    q = l2_normalize(q.reshape(B, S, GDN_HEADS, GDN_HEAD_DIM)) * (GDN_HEAD_DIM ** -0.5)
    k = l2_normalize(k.reshape(B, S, GDN_HEADS, GDN_HEAD_DIM))
    v = v.reshape(B, S, GDN_HEADS, GDN_HEAD_DIM)
    beta = jax.nn.sigmoid(b_raw.astype(jnp.float32))
    g = -jnp.exp(a_log.astype(jnp.float32)) * jax.nn.softplus(a_raw.astype(jnp.float32) + dt_bias.astype(jnp.float32))
    o = gated_delta_rule_chunked(q, k, v, g, beta)
    gate = jax.nn.silu(z.astype(jnp.float32)).reshape(B, S, GDN_HEADS, GDN_HEAD_DIM)
    o = rms_norm(o, o_gain) * gate
    return o.reshape(B, S, GDN_WIDTH).astype(q_raw.dtype)

def peer_ffn(h, w_query, sub_keys_1, sub_keys_2, expert_u, expert_v):
    B, S, D = h.shape
    hb = h.reshape(-1, PEER_TOKEN_BLOCK, D)

    def block(h_t):
        T = h_t.shape[0]
        q = jnp.einsum('td,dq->tq', h_t, w_query).reshape(T, PEER_HEADS, 2, PEER_HALF)
        s1 = jnp.einsum('thc,hkc->thk', q[:, :, 0], sub_keys_1)
        s2 = jnp.einsum('thc,hkc->thk', q[:, :, 1], sub_keys_2)
        v1, i1 = lax.top_k(s1, PEER_TOPK)
        v2, i2 = lax.top_k(s2, PEER_TOPK)
        cand_s = (v1[..., :, None] + v2[..., None, :]).reshape(T, PEER_HEADS, PEER_TOPK * PEER_TOPK)
        cand_i = (i1[..., :, None] * PEER_N_KEYS + i2[..., None, :]).reshape(T, PEER_HEADS, PEER_TOPK * PEER_TOPK)
        top_s, top_pos = lax.top_k(cand_s, PEER_TOPK)
        experts = jnp.take_along_axis(cand_i, top_pos, axis=-1).reshape(T, PEER_HEADS * PEER_TOPK)
        gates = jax.nn.softmax(top_s.astype(jnp.float32), axis=-1).reshape(T, PEER_HEADS * PEER_TOPK)
        u = expert_u[experts]
        act = jax.nn.gelu(jnp.einsum('td,tkd->tk', h_t, u).astype(jnp.float32), approximate=False)
        vv = expert_v[experts]
        return jnp.einsum('tk,tkd->td', (gates * act).astype(h_t.dtype), vv).astype(h_t.dtype)

    return lax.map(block, hb).reshape(B, S, D)

def setup_inputs(seed: int = 0) -> dict:
    key = jax.random.key(seed)
    ks = jax.random.split(key, 20)
    f32 = jnp.float32
    L = DEPTH
    x = jax.random.normal(ks[0], (BATCH, SEQ, D_MODEL), f32)
    norm_mix_gain = 1.0 + 0.1 * jax.random.normal(ks[1], (L, D_MODEL), f32)
    w_in = jax.random.normal(ks[2], (L, D_MODEL, IN_PROJ_COLS), f32) * D_MODEL ** -0.5
    conv_w = jax.random.normal(ks[3], (L, CONV_WIDTH, 3 * GDN_WIDTH), f32) * CONV_WIDTH ** -0.5
    a_log = jnp.log(jax.random.uniform(ks[4], (L, GDN_HEADS), f32, 1.0, 16.0))
    dt = jnp.exp(jax.random.uniform(ks[5], (L, GDN_HEADS), f32, float(np.log(1e-3)), float(np.log(1e-1))))
    dt_bias = dt + jnp.log(-jnp.expm1(-dt))
    gdn_out_gain = 1.0 + 0.1 * jax.random.normal(ks[6], (L, GDN_HEAD_DIM), f32)
    w_pool = jax.random.normal(ks[7], (L, POOL_GROUPS, POOL_GROUP_DIM, POOL_GROUP_DIM), f32) * POOL_GROUP_DIM ** -0.5
    b_pool = 0.01 * jax.random.normal(ks[8], (L, POOL_GROUPS, POOL_GROUP_DIM), f32)
    pool_scale = 1.0 + 0.1 * jax.random.normal(ks[9], (L, POOL_WIDTH), f32)
    w_out = jax.random.normal(ks[10], (L, MIX_WIDTH, D_MODEL), f32) * MIX_WIDTH ** -0.5
    norm_ffn_gain = 1.0 + 0.1 * jax.random.normal(ks[11], (L, D_MODEL), f32)
    peer_w_query = jax.random.normal(ks[12], (L, D_MODEL, PEER_HEADS * PEER_QUERY_DIM), f32) * D_MODEL ** -0.5
    peer_sub_keys_1 = jax.random.normal(ks[13], (L, PEER_HEADS, PEER_N_KEYS, PEER_HALF), f32) * PEER_HALF ** -0.5
    peer_sub_keys_2 = jax.random.normal(ks[14], (L, PEER_HEADS, PEER_N_KEYS, PEER_HALF), f32) * PEER_HALF ** -0.5
    peer_expert_u = jax.random.normal(ks[15], (L, PEER_N_EXPERTS, D_MODEL), f32) * D_MODEL ** -0.5
    peer_expert_v = jax.random.normal(ks[16], (L, PEER_N_EXPERTS, D_MODEL), f32) * 0.5
    norm_final_gain = 1.0 + 0.1 * jax.random.normal(ks[17], (D_MODEL,), f32)
    return {'x': x, 'norm_mix_gain': norm_mix_gain, 'w_in': w_in, 'conv_w': conv_w,
            'a_log': a_log, 'dt_bias': dt_bias, 'gdn_out_gain': gdn_out_gain,
            'w_pool': w_pool, 'b_pool': b_pool, 'pool_scale': pool_scale, 'w_out': w_out,
            'norm_ffn_gain': norm_ffn_gain, 'peer_w_query': peer_w_query,
            'peer_sub_keys_1': peer_sub_keys_1, 'peer_sub_keys_2': peer_sub_keys_2,
            'peer_expert_u': peer_expert_u, 'peer_expert_v': peer_expert_v,
            'norm_final_gain': norm_final_gain}

def reference(x, norm_mix_gain, w_in, conv_w, a_log, dt_bias, gdn_out_gain, w_pool, b_pool,
              pool_scale, w_out, norm_ffn_gain, peer_w_query, peer_sub_keys_1, peer_sub_keys_2,
              peer_expert_u, peer_expert_v, norm_final_gain):
    h = x
    for layer in range(DEPTH):
        hn = rms_norm(h, norm_mix_gain[layer])
        proj = jnp.einsum('bsd,dc->bsc', hn, w_in[layer])
        p_in, q_raw, k_raw, v_raw, z, b_raw, a_raw = jnp.split(proj, SPLIT_POINTS, axis=-1)
        pool_out = multiscale_pool_mixer(p_in, w_pool[layer], b_pool[layer], pool_scale[layer])
        gdn_out = gated_deltanet_mixer(q_raw, k_raw, v_raw, z, b_raw, a_raw, conv_w[layer],
                                       a_log[layer], dt_bias[layer], gdn_out_gain[layer])
        mixed = jnp.concatenate([pool_out, gdn_out], axis=-1)
        h = h + jnp.einsum('bsc,cd->bsd', mixed, w_out[layer]).astype(h.dtype)
        hf = rms_norm(h, norm_ffn_gain[layer])
        h = h + peer_ffn(hf, peer_w_query[layer], peer_sub_keys_1[layer], peer_sub_keys_2[layer],
                         peer_expert_u[layer], peer_expert_v[layer])
    return rms_norm(h, norm_final_gain)


_drawn_inputs = setup_inputs


def setup_inputs(seed=0):
    import zlib

    import numpy as np

    out = dict(_drawn_inputs(seed))
    spreads = {}
    factors = {'b_pool': 3.515}
    for name, (base, spread) in spreads.items():
        noise = np.random.default_rng([zlib.crc32(name.encode()), seed]).standard_normal(out[name].shape)
        drawn = base * np.exp(spread * noise) if base else spread * noise
        out[name] = jnp.asarray(drawn.astype(out[name].dtype))
    for name, factor in factors.items():
        out[name] = (out[name] * factor).astype(out[name].dtype)
    return out
```

```python
from contextlib import ExitStack, contextmanager

import numpy as np

import concourse.bass as bass
from concourse import mybir

P = 128
SEQ, DM = 1024, 1024
TILES = SEQ // P
DB = DM // P
CHUNK = 64
HALF = 512
HEADS = 4
HD = 128
POOL_WINDOWS = (2, 4, 8, 16)
PAD = 16
TAPS = 4
EPS = 1e-6
PHEADS, NKEYS, TOPK = 8, 128, 16
QD = 2 * P
PICKS = PHEADS * TOPK
LEVELS = (2, 4, 8, 16, 32)
RING = 8
GROUP = 4
LOW = -3.0e38


class Chain:

    def __init__(self, engine, sem):
        self.engine, self.sem, self.base, self.n = engine, sem, 0, 0

    def link(self, instruction):
        self.n += 1
        instruction.then_inc(self.sem, 1)
        self.engine.wait_ge(self.sem, self.base + self.n)

    @contextmanager
    def loop(self, count, links):
        base, n = self.base, self.n
        with self.engine.Fori(0, count) as i:
            self.base, self.n = i * links + (base + n), 0
            yield i
            assert self.n == links, f"the body makes {self.n} links"
        self.base, self.n = base, n + count * links


class Cut:

    def __init__(self, ap):
        self.ap, self.at = ap, 0

    def __call__(self, cols):
        self.at += cols
        assert self.at <= self.ap.shape[1], (self.at, self.ap.shape)
        return self.ap[:, self.at - cols:self.at]


def constants():
    j, i = np.arange(P)[:, None], np.arange(P)[None, :]
    same = (j // CHUNK) == (i // CHUNK)
    cols = [j == i, np.broadcast_to(np.arange(TOPK), (P, TOPK)),
            np.ones((P, P)), same & (j <= i), same & (j > i)]
    for s in (1,) + LEVELS:
        cols.append((j // (2 * s) == i // (2 * s)) & (j % (2 * s) < s) & (i % (2 * s) >= s))
    for w in POOL_WINDOWS:
        cols.append(np.broadcast_to(1.0 / np.minimum(np.arange(PAD) + 1, w), (P, PAD)))
    return np.concatenate([c.astype(np.float32) for c in cols], axis=1)


N_KEPT = P + TOPK
N_MASKS = (3 + 1 + len(LEVELS)) * P + len(POOL_WINDOWS) * PAD


def build(nc, a, out):
    F32, I32, U32 = mybir.dt.float32, mybir.dt.int32, mybir.dt.uint32
    ALU, ACT, AX = mybir.AluOpType, mybir.ActivationFunctionType, mybir.AxisListType
    PE, V, A, G = nc.tensor, nc.vector, nc.scalar, nc.gpsimd
    ds = bass.ds
    top = ExitStack()

    def sb(name, cols, dtype=F32):
        return top.enter_context(nc.sbuf_tensor(name, [P, cols], dtype))[:, :]

    def sem(name):
        return top.enter_context(nc.semaphore(name))

    def per_head(ap):
        return ap.rearrange("p (h c) -> p h c", h=HEADS)

    def over_heads(ap):
        return ap.unsqueeze(1).to_broadcast([P, HEADS, P])

    def over_cols(ap, cols=P):
        return ap.unsqueeze(2).to_broadcast([ap.shape[0], ap.shape[1], cols])

    with top:
        bank = [top.enter_context(nc.psum_tensor(f"bank{n}", [P, HALF], F32))[:, :] for n in range(8)]
        pool_steps = sem("pool_steps")
        vc, ac = Chain(V, sem("vector_chain")), Chain(A, sem("scalar_chain"))

        kept = sb("kept", N_KEPT)
        ident, iota = kept[:, 0:P], kept[:, P:P + TOPK]
        h_all = sb("h_all", TILES * DM)
        sub_keys = sb("sub_keys", 2 * PHEADS * NKEYS)
        gain_ffn = sb("gain_ffn", DM)
        gain_fin = sb("gain_fin", DM)
        stat = sb("stat", 32)
        eps_col = sb("eps_col", 2)
        late = sb("late", 2 * 8 * DM)
        ring_mem = sb("ring_mem", RING * 2 * DM)
        work = sb("work", 7900)

        w_query = late
        qkv_t = late[:, 0:12 * SEQ]
        z_all = ring_mem[:, 0:TILES * HALF]
        o_all = ring_mem[:, TILES * HALF:2 * TILES * HALF]
        hn_t = ring_mem[:, 2 * TILES * HALF:2 * TILES * HALF + DB * SEQ]

        mix = Cut(work)
        masks = mix(N_MASKS)
        ones, causal, after = (masks[:, n * P:(n + 1) * P] for n in range(3))
        level_mask = [masks[:, (3 + n) * P:(4 + n) * P] for n in range(6)]
        inv_count = masks[:, 9 * P:]
        small = mix(64)
        conv_w, b_pool, pool_scale = small[:, 0:48], small[:, 48:52], small[:, 52:56]
        a_log, dt_bias = small[:, 56:60], small[:, 60:64]
        out_gain = mix(HD)
        ab_all = mix(TILES * 8)
        pool_t = mix(4 * SEQ)

        early = Cut(late)
        wz, wab, gain_mix, hn, hn_tile, junk = early(DB * HALF), early(DB * 8), early(DM), early(DM), early(DM), early(DM)
        x_in, const_in, wz_in, small_in, keys_in = (sem(n) for n in ("x_in", "const_in", "wz_in", "small_in", "keys_in"))
        sq_made, ms_made, root_made, rstd_made = (sem(n) for n in ("sumsq_made", "mean_made", "root_made", "rstd_made"))
        hn_made, turned, tile_kept, z_made, z_kept, hn_kept = (
            sem(n) for n in ("hn_made", "hn_turned", "hn_tile_kept", "z_made", "z_kept", "hn_kept"))
        with nc.Block() as block:
            @block.sync
            def _(sp):
                sp.dma_start(h_all.rearrange("p (t d) -> p t d", t=TILES),
                             a["x"].rearrange("(t p) d -> p t d", p=P)).then_inc(x_in, 16)
                sp.dma_start(kept, a["constants"][:, 0:N_KEPT]).then_inc(const_in, 16)
                sp.dma_start(gain_mix, a["gain_mix"].partition_broadcast(P)).then_inc(const_in, 16)
                sp.dma_start(wz, a["wz"]).then_inc(wz_in, 16)
                sp.dma_start(wab, a["wab"]).then_inc(wz_in, 16)
                sp.dma_start(masks, a["constants"][:, N_KEPT:]).then_inc(small_in, 16)
                sp.dma_start(small[:, 0:56], a["per_channel"]).then_inc(small_in, 16)
                sp.dma_start(small[:, 56:64], a["per_head"].partition_broadcast(P)).then_inc(small_in, 16)
                sp.dma_start(out_gain, a["out_gain"].partition_broadcast(P)).then_inc(small_in, 16)
                sp.dma_start(gain_ffn, a["gain_ffn"].partition_broadcast(P)).then_inc(keys_in, 16)
                sp.dma_start(gain_fin, a["gain_fin"].partition_broadcast(P)).then_inc(keys_in, 16)
                sp.dma_start(sub_keys, a["sub_keys"]).then_inc(keys_in, 16)

            @block.scalar
            def _(act):
                act.wait_ge(x_in, 16)
                with act.Fori(0, TILES) as t:
                    A.activation(junk, h_all[:, ds(t * DM, DM)], ACT.Square,
                                 accum_out=stat[:, ds(t, 1)]).then_inc(sq_made, 1)
                    act.wait_ge(sq_made, t + 1)
                act.wait_ge(ms_made, 1)
                A.activation(stat[:, 16:24], stat[:, 8:16], ACT.Sqrt).then_inc(root_made, 1)
                with act.Fori(0, TILES) as t:
                    act.wait_ge(turned, t + 1)
                    act.wait_ge(z_made, t)
                    act.wait_ge(hn_kept, t)
                    A.activation(hn_tile[:, 0:HALF], bank[0], ACT.Copy)
                    A.activation(hn_tile[:, HALF:DM], bank[1], ACT.Copy).then_inc(tile_kept, 1)
                    act.wait_ge(z_made, t + 1)
                    A.activation(z_all[:, ds(t * HALF, HALF)], bank[2], ACT.Copy)
                    A.activation(ab_all[:, ds(t * 8, 8)], bank[3][:, 0:8], ACT.Copy).then_inc(z_kept, 1)

            @block.vector
            def _(dve):
                V.memset(eps_col[:, 0:1], EPS * HD)
                V.memset(eps_col[:, 1:2], EPS)
                dve.wait_ge(sq_made, TILES)
                V.tensor_scalar(stat[:, 8:16], stat[:, 0:8], 1.0 / DM, EPS, ALU.mult, ALU.add).then_inc(ms_made, 1)
                dve.wait_ge(root_made, 1)
                V.reciprocal(stat[:, 24:32], stat[:, 16:24]).then_inc(rstd_made, 1)
                dve.wait_ge(rstd_made, 1)
                dve.wait_ge(const_in, 32)
                with dve.Fori(0, TILES) as t:
                    dve.wait_ge(turned, t)
                    V.scalar_tensor_tensor(hn, h_all[:, ds(t * DM, DM)], stat[:, ds(t + 24, 1)],
                                           gain_mix, ALU.mult, ALU.mult).then_inc(hn_made, 1)

            @block.tensor
            def _(pe):
                pe.wait_ge(const_in, 32)
                pe.wait_ge(wz_in, 32)
                with pe.Fori(0, TILES) as t:
                    pe.wait_ge(hn_made, t + 1)
                    pe.wait_ge(tile_kept, t)
                    for d in range(DB):
                        m = PE.transpose(bank[d // 4][:, (d % 4) * P:(d % 4 + 1) * P], hn[:, d * P:(d + 1) * P], ident)
                    m.then_inc(turned, 1)
                    pe.wait_ge(tile_kept, t + 1)
                    pe.wait_ge(z_kept, t)
                    for d in range(DB):
                        PE.matmul(bank[2], hn_tile[:, d * P:(d + 1) * P], wz[:, d * HALF:(d + 1) * HALF],
                                  start=(d == 0), stop=(d == DB - 1))
                    for d in range(DB):
                        m = PE.matmul(bank[3][:, 0:8], hn_tile[:, d * P:(d + 1) * P], wab[:, d * 8:(d + 1) * 8],
                                      start=(d == 0), stop=(d == DB - 1))
                    m.then_inc(z_made, 1)

            @block.gpsimd
            def _(pool):
                with pool.Fori(0, TILES) as t:
                    pool.wait_ge(tile_kept, t + 1)
                    pool.sem_inc(pool_steps, 1)
                    G.tensor_copy(hn_t.rearrange("p (d s) -> p d s", d=DB)[:, :, ds(t * P, P)],
                                  hn_tile.rearrange("p (d s) -> p d s", d=DB)).then_inc(hn_kept, 1)

        wc = [late[:, 12 * SEQ + n * DM:12 * SEQ + (n + 1) * DM] for n in range(4)]
        spare, rest = Cut(o_all), Cut(work[:, mix.at:])
        raw = [spare(PAD + SEQ), spare(PAD + SEQ)]
        y = [spare(PAD + SEQ), rest(PAD + SEQ)]
        diff = rest(SEQ)
        w_pool = spare(4 * P)
        wc_in = [sem(f"wc_in{n}") for n in range(4)]
        pool_w_in, proj_made, raw_kept, sums_made, silu_made, pooled, pool_kept, pads_made = (
            sem(n) for n in ("pool_w_in", "proj_made", "raw_kept", "sums_made", "silu_made", "pooled", "pool_kept", "pads_made"))
        with nc.Block() as block:
            @block.sync
            def _(sp):
                for s in range(4):
                    sp.dma_start(wc[s], a["wc"][s, :, :]).then_inc(wc_in[s], 16)
                sp.dma_start(w_pool, a["w_pool"]).then_inc(pool_w_in, 16)
                with sp.Fori(0, 3) as i:
                    for s in range(4):
                        sp.wait_ge(proj_made, i * 8 + (2 * s + 2))
                        sp.dma_start(wc[s], a["wc"][ds(i * 4 + (4 + s), 1), :, :].rearrange("a p c -> p (a c)")).then_inc(wc_in[s], 16)

            @block.tensor
            def _(pe):
                def project(s, loaded, before):
                    pe.wait_ge(wc_in[s], loaded)
                    for half in range(2):
                        if before is not None:
                            pe.wait_ge(raw_kept, before + half)
                        for d in range(DB):
                            m = PE.matmul(bank[2 * (s % 2) + half], wc[s][:, d * P:(d + 1) * P],
                                          hn_t[:, d * SEQ + half * HALF:d * SEQ + (half + 1) * HALF],
                                          start=(d == 0), stop=(d == DB - 1))
                        m.then_inc(proj_made, 1)

                def pool_product(g):
                    pe.wait_ge(sums_made, g + 1)
                    if g > 0:
                        pe.wait_ge(pool_kept, 2 * g)
                    for half in range(2):
                        PE.matmul(bank[4 + half], w_pool[:, g * P:(g + 1) * P], diff[:, half * HALF:(half + 1) * HALF],
                                  start=True, stop=True).then_inc(pooled, 1)

                project(0, 16, None)
                project(1, 16, None)
                pe.wait_ge(pool_w_in, 16)
                pool_product(0)
                project(2, 16, 1)
                pool_product(1)
                project(3, 16, 3)
                pool_product(2)
                pool_product(3)
                with pe.Fori(0, 3) as i:
                    for s in range(4):
                        project(s, i * 16 + 32, i * 8 + (2 * s + 5))

            @block.scalar
            def _(act):
                def keep_raw(s, made, read):
                    for half in range(2):
                        act.wait_ge(proj_made, made + half)
                        if half == 0 and read is not None:
                            act.wait_ge(sums_made, read)
                        A.activation(raw[s % 2][:, PAD + half * HALF:PAD + (half + 1) * HALF],
                                     bank[2 * (s % 2) + half], ACT.Copy).then_inc(raw_kept, 1)

                act.wait_ge(pads_made, 1)
                for s in range(4):
                    keep_raw(s, 2 * s + 1, s - 1 if s >= 2 else None)
                with act.Fori(0, 3) as i:
                    for s in range(4):
                        keep_raw(s, i * 8 + (2 * s + 9), i * 4 + (s + 3))
                        act.wait_ge(sums_made, i * 4 + (s + 5))
                        A.activation(qkv_t[:, ds(i * (4 * SEQ) + s * SEQ, SEQ)], y[s % 2][:, PAD:],
                                     ACT.Silu).then_inc(silu_made, 1)

            @block.vector
            def _(dve):
                def pool_out(g):
                    for half in range(2):
                        dve.wait_ge(pooled, 2 * g + half + 1)
                        V.tensor_scalar(pool_t[:, g * SEQ + half * HALF:g * SEQ + (half + 1) * HALF], bank[4 + half],
                                        b_pool[:, g:g + 1], pool_scale[:, g:g + 1], ALU.add, ALU.mult).then_inc(pool_kept, 1)

                dve.wait_ge(pads_made, 1)
                dve.wait_ge(small_in, 64)
                for g, window in enumerate(POOL_WINDOWS):
                    dve.wait_ge(raw_kept, 2 * g + 2)
                    src, reach, n = raw[g % 2], 1, 0
                    while reach < window:
                        dst = y[n % 2]
                        vc.link(V.tensor_tensor(dst[:, PAD:], src[:, PAD:], src[:, PAD - reach:PAD + SEQ - reach], ALU.add))
                        src, reach, n = dst, 2 * reach, n + 1
                    if g > 0:
                        dve.wait_ge(pooled, 2 * g)
                    vc.link(V.scalar_tensor_tensor(diff, src[:, PAD:], 1.0 / window, raw[g % 2][:, PAD:], ALU.mult, ALU.subtract))
                    vc.link(V.tensor_tensor(diff[:, 0:PAD], src[:, PAD:2 * PAD], inv_count[:, g * PAD:(g + 1) * PAD], ALU.mult))
                    V.tensor_tensor(diff[:, 0:PAD], diff[:, 0:PAD], raw[g % 2][:, PAD:2 * PAD], ALU.subtract).then_inc(sums_made, 1)
                    dve.wait_ge(sums_made, g + 1)
                    if g > 0:
                        pool_out(g - 1)
                pool_out(3)
                with vc.loop(3, 4 * (TAPS - 1)) as i:
                    for s in range(4):
                        dve.wait_ge(raw_kept, i * 8 + (2 * s + 10))
                        dst = y[s % 2][:, PAD:]
                        taps = [small[:, ds(i * 16 + (4 * s + k), 1)] for k in range(TAPS)]
                        dve.wait_ge(silu_made, i * 4 + max(s - 1, 0))
                        vc.link(V.tensor_scalar(dst, raw[s % 2][:, PAD:], taps[TAPS - 1], None, ALU.mult))
                        for k in range(1, TAPS):
                            m = V.scalar_tensor_tensor(dst, raw[s % 2][:, PAD - k:PAD + SEQ - k], taps[TAPS - 1 - k], dst, ALU.mult, ALU.add)
                            if k < TAPS - 1:
                                vc.link(m)
                            else:
                                m.then_inc(sums_made, 1)
                                dve.wait_ge(sums_made, i * 4 + (s + 5))

            @block.gpsimd
            def _(pool):
                for buf in (raw[0], raw[1], y[0]):
                    G.memset(buf[:, 0:PAD], 0.0)
                G.memset(y[1][:, 0:PAD], 0.0).then_inc(pads_made, 1)

        cut = Cut(hn_t)
        square = [cut(SEQ), cut(SEQ)]
        root = [cut(SEQ), cut(SEQ)]
        square_made, square_sum, norm_root, normed = (sem(n) for n in ("square_made", "square_sum", "norm_root", "qk_normed"))
        with nc.Block() as block:
            @block.scalar
            def _(act):
                for q_or_k, scale in enumerate((float(HD), 1.0)):
                    with act.Fori(0, HEADS // 2) as i:
                        for s in range(2):
                            before = i * 2 + (4 * q_or_k + s)
                            src = qkv_t[:, ds(i * (2 * SEQ) + (4 * q_or_k + s) * SEQ, SEQ)]
                            A.activation(square[s], src, ACT.Square).then_inc(square_made, 1)
                            act.wait_ge(square_sum, before + 1)
                            act.wait_ge(normed, i * 2 + (4 * q_or_k))
                            for half in range(2):
                                m = A.activation(root[s][:, half * HALF:(half + 1) * HALF], bank[2 * s + half], ACT.Sqrt,
                                                 scale=scale, bias=eps_col[:, q_or_k:q_or_k + 1])
                            m.then_inc(norm_root, 1)

            @block.tensor
            def _(pe):
                with pe.Fori(0, HEADS) as i:
                    for s in range(2):
                        pe.wait_ge(square_made, i * 2 + (s + 1))
                        pe.wait_ge(norm_root, i * 2 + 0)
                        for half in range(2):
                            m = PE.matmul(bank[2 * s + half], ones, square[s][:, half * HALF:(half + 1) * HALF], start=True, stop=True)
                        m.then_inc(square_sum, 1)

            @block.vector
            def _(dve):
                with vc.loop(HEADS, 2) as i:
                    for s in range(2):
                        dve.wait_ge(norm_root, i * 2 + (s + 1))
                        vc.link(V.reciprocal(root[s], root[s]))
                        at = qkv_t[:, ds(i * (2 * SEQ) + s * SEQ, SEQ)]
                        V.tensor_tensor(at, at, root[s], ALU.mult).then_inc(normed, 1)

        TH = TILES * HEADS
        cut = Cut(work[:, mix.at:])
        log_dec, log_sum, beta, beta_dec, dec_end, sp_a, sp_b, sp_c = (cut(TH) for _ in range(8))
        exp_sum = sp_a
        b_raw = ab_all.rearrange("p (t c) -> p t c", t=TILES)[:, :, 0:HEADS]
        a_raw = ab_all.rearrange("p (t c) -> p t c", t=TILES)[:, :, HEADS:2 * HEADS]

        def by_tile(ap):
            return ap.rearrange("p (t h) -> p t h", t=TILES)

        def over_tiles(ap):
            return ap.unsqueeze(1).to_broadcast([P, TILES, HEADS])

        soft_in, soft_e, soft_l, dec_made, sums_done, exps_done = (
            sem(n) for n in ("softplus_in", "softplus_exp", "softplus_log", "log_decay_made", "decay_sums_made", "decay_exps_made"))
        with nc.Block() as block:
            @block.vector
            def _(dve):
                vc.link(V.tensor_tensor(by_tile(sp_a), a_raw, over_tiles(dt_bias), ALU.add))
                vc.link(V.tensor_scalar(sp_b, sp_a, -1.0, None, ALU.mult))
                V.tensor_tensor(sp_b, sp_b, sp_a, ALU.min).then_inc(soft_in, 1)
                dve.wait_ge(soft_e, 3)
                vc.link(V.tensor_scalar(beta, beta, 1.0, None, ALU.add))
                vc.link(V.reciprocal(beta, beta))
                dve.wait_ge(soft_l, 1)
                vc.link(V.scalar_tensor_tensor(sp_c, sp_a, 0.0, sp_c, ALU.max, ALU.add))
                V.scalar_tensor_tensor(by_tile(log_dec), by_tile(sp_c), -1.0, over_tiles(stat[:, 0:HEADS]), ALU.mult, ALU.mult).then_inc(dec_made, 1)
                dve.wait_ge(exps_done, 1)
                vc.link(V.tensor_copy(log_sum, bank[0][:, 0:TH]))
                vc.link(V.tensor_tensor(beta_dec, beta, exp_sum, ALU.mult))

            @block.scalar
            def _(act):
                A.activation(stat[:, 0:HEADS], a_log, ACT.Exp).then_inc(soft_e, 1)
                A.activation(by_tile(beta), b_raw, ACT.Exp, scale=-1.0).then_inc(soft_e, 1)
                act.wait_ge(soft_in, 1)
                A.activation(sp_b, sp_b, ACT.Exp).then_inc(soft_e, 1)
                act.wait_ge(soft_e, 3)
                A.activation(sp_c, sp_b, ACT.Ln, bias=1.0).then_inc(soft_l, 1)
                act.wait_ge(sums_done, 1)
                A.activation(exp_sum, bank[0][:, 0:TH], ACT.Exp)
                A.activation(dec_end, bank[0][:, TH:2 * TH], ACT.Exp).then_inc(exps_done, 1)

            @block.tensor
            def _(pe):
                pe.wait_ge(dec_made, 1)
                PE.matmul(bank[0][:, 0:TH], causal, log_dec, start=True, stop=True)
                PE.matmul(bank[0][:, TH:2 * TH], after, log_dec, start=True, stop=True).then_inc(sums_done, 1)

        pieces = [hn_t[:, n * HALF:(n + 1) * HALF] for n in range(16)]
        pieces += [late[:, 12 * SEQ + n * HALF:12 * SEQ + (n + 1) * HALF] for n in range(8)]
        pieces += [cut(HALF) for _ in range(3)]
        (sum_rhs, beta_rhs, k_tile, v_tile, dec, row_dec, solve, scores, q_first, q_second, v_beta, k_beta, k_first, k_second,
         inv, inv_t, prod, u_tile, w_tile, v_new, state, middle) = pieces[:22]
        lower = pieces[22:27]
        q_all, k_all, v_all = (qkv_t[:, n * 4 * SEQ:(n + 1) * 4 * SEQ].rearrange("p (h s) -> p h s", h=HEADS) for n in range(3))
        names = ("zeroed", "kv_kept", "sum_rhs_made", "beta_rhs_made", "rows_made", "kk_made", "turned_kv", "diff_made", "rows_exp",
                 "solve_made", "lower_made", "inv_t_made", "inv_turned", "inv_made", "prod_made", "prod_kept", "corr_made", "level_done",
                 "tokens_made", "uw_made", "uw_kept", "ws_made", "v_new_made", "gain_made", "state_made", "o_made", "o_kept")
        S = {n: sem("d_" + n) for n in names}
        NL = len(LEVELS)
        with nc.Block() as block:
            @block.gpsimd
            def _(pool):
                for buf in (state, v_new, q_first, q_second, k_first):
                    G.memset(buf, 0.0)
                G.memset(k_second, 0.0).then_inc(S["zeroed"], 1)
                with pool.Fori(0, TILES) as t:
                    pool.wait_ge(S["rows_made"], t)
                    pool.sem_inc(pool_steps, 1)
                    G.tensor_tensor(per_head(beta_rhs), over_heads(ident), over_cols(beta[:, ds(t * HEADS, HEADS)]), ALU.mult).then_inc(S["beta_rhs_made"], 1)
                    pool.wait_ge(S["solve_made"], t + 1)
                    pool.wait_ge(S["level_done"], t * NL)
                    for n in range(NL):
                        G.tensor_tensor(per_head(lower[n]), per_head(solve), over_heads(level_mask[n + 1]), ALU.mult).then_inc(S["lower_made"], 1)

            @block.scalar
            def _(act):
                with act.Fori(0, TILES) as t:
                    act.wait_ge(S["turned_kv"], t)
                    A.activation(per_head(k_tile), k_all[:, :, ds(t * P, P)], ACT.Copy)
                    A.activation(per_head(v_tile), v_all[:, :, ds(t * P, P)], ACT.Copy).then_inc(S["kv_kept"], 1)
                    act.wait_ge(S["diff_made"], t + 1)
                    act.wait_ge(S["state_made"], t * 2)
                    A.activation(row_dec, bank[0], ACT.Exp).then_inc(S["rows_exp"], 1)
                    A.activation(dec, dec, ACT.Exp).then_inc(S["rows_exp"], 1)
                    act.wait_ge(S["inv_turned"], t + 1)
                    A.activation(inv, bank[6], ACT.Copy).then_inc(S["inv_made"], 1)
                    for n in range(NL):
                        act.wait_ge(S["prod_made"], t * NL + n + 1)
                        A.activation(prod, bank[6], ACT.Copy).then_inc(S["prod_kept"], 1)
                    act.wait_ge(S["uw_made"], t + 1)
                    A.activation(u_tile, bank[2], ACT.Copy)
                    A.activation(w_tile, bank[3], ACT.Copy).then_inc(S["uw_kept"], 1)
                    act.wait_ge(S["o_made"], t + 1)
                    A.activation(o_all[:, ds(t * HALF, HALF)], bank[7], ACT.Copy).then_inc(S["o_kept"], 1)

            @block.vector
            def _(dve):
                dve.wait_ge(S["zeroed"], 1)
                with vc.loop(TILES, 5) as t:
                    four = ds(t * HEADS, HEADS)
                    dve.wait_ge(S["rows_made"], t)
                    V.tensor_tensor(per_head(sum_rhs), over_heads(causal), over_cols(log_dec[:, four]), ALU.mult).then_inc(S["sum_rhs_made"], 1)
                    dve.wait_ge(S["rows_made"], t + 1)
                    vc.link(V.tensor_tensor(per_head(dec), per_head(bank[0]), over_cols(log_sum[:, four]), ALU.subtract))
                    V.tensor_tensor(per_head(dec), per_head(dec), over_heads(causal), ALU.mult).then_inc(S["diff_made"], 1)
                    dve.wait_ge(S["rows_exp"], t * 2 + 2)
                    vc.link(V.tensor_tensor(per_head(dec), per_head(dec), over_heads(causal), ALU.mult))
                    dve.wait_ge(S["kk_made"], t + 1)
                    dve.wait_ge(S["lower_made"], t * NL)
                    dve.wait_ge(S["o_made"], t)
                    vc.link(V.tensor_tensor(solve, bank[2], dec, ALU.mult))
                    V.tensor_tensor(solve, solve, bank[1], ALU.mult).then_inc(S["solve_made"], 1)
                    vc.link(V.tensor_tensor(scores, bank[3], dec, ALU.mult))
                    dve.wait_ge(S["solve_made"], t + 1)
                    vc.link(V.tensor_tensor(per_head(inv_t), per_head(solve), over_heads(level_mask[0]), ALU.mult))
                    V.tensor_tensor(per_head(inv_t), over_heads(ident), per_head(inv_t), ALU.subtract).then_inc(S["inv_t_made"], 1)
                    dve.wait_ge(S["turned_kv"], t + 1)
                    V.tensor_tensor(per_head(v_beta), per_head(bank[5]), over_cols(beta[:, four]), ALU.mult)
                    V.tensor_tensor(per_head(k_beta), per_head(bank[4]), over_cols(beta_dec[:, four]), ALU.mult)
                    for c, (qd, kd) in enumerate(((q_first, k_first), (q_second, k_second))):
                        of = slice(c * CHUNK, (c + 1) * CHUNK)
                        V.tensor_tensor(per_head(kd)[of], per_head(bank[4])[of], over_cols(dec_end[of, four]), ALU.mult)
                        m = V.tensor_tensor(per_head(qd)[:, :, of], q_all[:, :, ds(t * P + c * CHUNK, CHUNK)], per_head(row_dec)[:, :, of], ALU.mult)
                    m.then_inc(S["tokens_made"], 1)
                    dve.wait_ge(S["inv_made"], t + 1)
                    for n in range(NL):
                        dve.wait_ge(S["corr_made"], t * NL + n + 1)
                        if n < NL - 1:
                            V.tensor_tensor(inv, inv, bank[7], ALU.subtract)
                        V.tensor_tensor(inv_t, inv_t, bank[6], ALU.subtract).then_inc(S["level_done"], 1)
                        dve.wait_ge(S["level_done"], t * NL + n + 1)
                    dve.wait_ge(S["uw_kept"], t + 1)
                    for c, (old, new) in enumerate(((state, middle), (middle, state))):
                        of = slice(c * CHUNK, (c + 1) * CHUNK)
                        dve.wait_ge(S["ws_made"], t * 2 + c + 1)
                        V.tensor_tensor(v_new[of], u_tile[of], bank[4][of], ALU.subtract).then_inc(S["v_new_made"], 1)
                        dve.wait_ge(S["gain_made"], t * 2 + c + 1)
                        if c == 1:
                            dve.wait_ge(S["o_made"], t + 1)
                        end = (c + 1) * CHUNK - 1
                        for h in range(HEADS):
                            cols = slice(h * P, (h + 1) * P)
                            m = V.scalar_tensor_tensor(new[:, cols], old[:, cols], row_dec[:, h * P + end:h * P + end + 1],
                                                       bank[5][:, cols], ALU.mult, ALU.add)
                        m.then_inc(S["state_made"], 1)
                        dve.wait_ge(S["state_made"], t * 2 + c + 1)

            @block.tensor
            def _(pe):
                def heads(to, left, right):
                    for h in range(HEADS):
                        c = slice(h * P, (h + 1) * P)
                        m = PE.matmul(to[:, c], left[:, c], right[:, c], start=True, stop=True)
                    return m

                def turn(to, of):
                    for h in range(HEADS):
                        c = slice(h * P, (h + 1) * P)
                        m = PE.transpose(to[:, c], of[:, c], ident)
                    return m

                pe.wait_ge(S["zeroed"], 1)
                with pe.Fori(0, TILES) as t:
                    pe.wait_ge(S["sum_rhs_made"], t + 1)
                    pe.wait_ge(S["beta_rhs_made"], t + 1)
                    pe.wait_ge(S["state_made"], t * 2)
                    pe.wait_ge(S["o_kept"], t)
                    PE.matmul(bank[0], ones, sum_rhs, start=True, stop=True)
                    PE.matmul(bank[1], ones, beta_rhs, start=True, stop=True).then_inc(S["rows_made"], 1)
                    pe.wait_ge(S["kv_kept"], t + 1)
                    heads(bank[2], k_tile, k_tile)
                    for h in range(HEADS):
                        c = slice(h * P, (h + 1) * P)
                        m = PE.matmul(bank[3][:, c], k_tile[:, c], q_all[:, h, ds(t * P, P)], start=True, stop=True)
                    m.then_inc(S["kk_made"], 1)
                    turn(bank[4], k_tile)
                    turn(bank[5], v_tile).then_inc(S["turned_kv"], 1)
                    pe.wait_ge(S["inv_t_made"], t + 1)
                    turn(bank[6], inv_t).then_inc(S["inv_turned"], 1)
                    pe.wait_ge(S["inv_made"], t + 1)
                    for n in range(NL):
                        pe.wait_ge(S["lower_made"], t * NL + n + 1)
                        pe.wait_ge(S["level_done"], t * NL + n)
                        heads(bank[6], lower[n], inv).then_inc(S["prod_made"], 1)
                        pe.wait_ge(S["prod_kept"], t * NL + n + 1)
                        if n < NL - 1:
                            heads(bank[7], inv_t, prod)
                        heads(bank[6], prod, inv_t).then_inc(S["corr_made"], 1)
                    pe.wait_ge(S["level_done"], t * NL + NL)
                    pe.wait_ge(S["tokens_made"], t + 1)
                    heads(bank[2], inv_t, v_beta)
                    heads(bank[3], k_beta, inv_t).then_inc(S["uw_made"], 1)
                    pe.wait_ge(S["uw_kept"], t + 1)
                    for c, (old, k_chunk) in enumerate(((state, k_first), (middle, k_second))):
                        if c == 1:
                            pe.wait_ge(S["state_made"], t * 2 + 1)
                        heads(bank[4], w_tile, old).then_inc(S["ws_made"], 1)
                        pe.wait_ge(S["v_new_made"], t * 2 + c + 1)
                        heads(bank[5], k_chunk, v_new).then_inc(S["gain_made"], 1)
                    for h in range(HEADS):
                        c = slice(h * P, (h + 1) * P)
                        PE.matmul(bank[7][:, c], q_first[:, c], state[:, c], start=True, stop=False)
                        PE.matmul(bank[7][:, c], q_second[:, c], middle[:, c], start=False, stop=False)
                        m = PE.matmul(bank[7][:, c], scores[:, c], v_new[:, c], start=False, stop=True)
                    m.then_inc(S["o_made"], 1)

        w_out = hn_t
        cut = Cut(work[:, mix.at:])
        squares, gated, mixed_g, mixed_p = cut(HALF), cut(HALF), cut(HALF), cut(HALF)
        o_stat = cut(3 * TH)
        w_out_in, w_query_in = sem("w_out_in"), sem("w_query_in")
        names = ("squares", "squares_used", "means", "roots", "rstds", "z_silu", "gated", "turned", "turned_kept", "pool_kept", "projected", "summed")
        M = {n: sem("m_" + n) for n in names}
        with nc.Block() as block:
            @block.sync
            def _(sp):
                sp.dma_start(w_out, a["w_out"]).then_inc(w_out_in, 16)
                sp.dma_start(w_query, a["w_query"]).then_inc(w_query_in, 16)

            @block.scalar
            def _(act):
                with act.Fori(0, TILES) as t:
                    act.wait_ge(M["squares_used"], t)
                    A.activation(squares, o_all[:, ds(t * HALF, HALF)], ACT.Square).then_inc(M["squares"], 1)
                act.wait_ge(M["means"], 1)
                A.activation(o_stat[:, TH:2 * TH], o_stat[:, 0:TH], ACT.Sqrt).then_inc(M["roots"], 1)
                with act.Fori(0, TILES) as t:
                    at = z_all[:, ds(t * HALF, HALF)]
                    A.activation(at, at, ACT.Silu).then_inc(M["z_silu"], 1)
                    act.wait_ge(M["turned"], t + 1)
                    act.wait_ge(M["projected"], t)
                    A.activation(mixed_g, bank[2], ACT.Copy).then_inc(M["turned_kept"], 1)

            @block.vector
            def _(dve):
                with vc.loop(TILES, 0) as t:
                    dve.wait_ge(M["squares"], t + 1)
                    V.tensor_reduce(o_stat[:, ds(t * HEADS, HEADS)], per_head(squares), AX.X, ALU.add).then_inc(M["squares_used"], 1)
                dve.wait_ge(M["squares_used"], TILES)
                V.tensor_scalar(o_stat[:, 0:TH], o_stat[:, 0:TH], 1.0 / HD, EPS, ALU.mult, ALU.add).then_inc(M["means"], 1)
                dve.wait_ge(M["roots"], 1)
                V.reciprocal(o_stat[:, 2 * TH:3 * TH], o_stat[:, TH:2 * TH]).then_inc(M["rstds"], 1)
                dve.wait_ge(M["rstds"], 1)
                with vc.loop(TILES, 2) as t:
                    dve.wait_ge(M["turned"], t)
                    vc.link(V.tensor_tensor(per_head(gated), per_head(o_all[:, ds(t * HALF, HALF)]), over_cols(o_stat[:, ds(t * HEADS + 2 * TH, HEADS)]), ALU.mult))
                    vc.link(V.tensor_tensor(per_head(gated), per_head(gated), over_heads(out_gain), ALU.mult))
                    dve.wait_ge(M["z_silu"], t + 1)
                    V.tensor_tensor(gated, gated, z_all[:, ds(t * HALF, HALF)], ALU.mult).then_inc(M["gated"], 1)
                    dve.wait_ge(M["projected"], t + 1)
                    for half in range(2):
                        at = h_all[:, ds(t * DM + half * HALF, HALF)]
                        m = V.tensor_tensor(at, bank[half], at, ALU.add)
                    m.then_inc(M["summed"], 1)
                    dve.wait_ge(M["summed"], t + 1)

            @block.tensor
            def _(pe):
                pe.wait_ge(w_out_in, 16)
                with pe.Fori(0, TILES) as t:
                    pe.wait_ge(M["gated"], t + 1)
                    pe.wait_ge(M["turned_kept"], t)
                    for h in range(HEADS):
                        c = slice(h * P, (h + 1) * P)
                        m = PE.transpose(bank[2][:, c], gated[:, c], ident)
                    m.then_inc(M["turned"], 1)
                    pe.wait_ge(M["turned_kept"], t + 1)
                    pe.wait_ge(M["pool_kept"], t + 1)
                    pe.wait_ge(M["summed"], t)
                    for half in range(2):
                        for d in range(DB):
                            src = mixed_p if d < 4 else mixed_g
                            m = PE.matmul(bank[half], src[:, (d % 4) * P:(d % 4 + 1) * P],
                                          w_out[:, d * DM + half * HALF:d * DM + (half + 1) * HALF], start=(d == 0), stop=(d == DB - 1))
                    m.then_inc(M["projected"], 1)

            @block.gpsimd
            def _(pool):
                with pool.Fori(0, TILES) as t:
                    pool.wait_ge(M["projected"], t)
                    pool.sem_inc(pool_steps, 1)
                    G.tensor_copy(per_head(mixed_p), pool_t.rearrange("p (g s) -> p g s", g=4)[:, :, ds(t * P, P)]).then_inc(M["pool_kept"], 1)

        cut = Cut(work)
        hf_now, hf_next, hf_t = cut(DM), cut(DM), cut(DM)
        q_head, q_head_t = cut(QD), cut(QD)
        diag = [cut(P) for _ in range(RING)]
        picks = cut(TILES * PICKS).bitcast(I32)
        pick_now = cut(TOPK).bitcast(I32)
        top_val, gates = cut(PICKS), cut(PICKS)
        val, ix, ix_f = cut(2 * TOPK), cut(2 * TOPK).bitcast(U32), cut(2 * TOPK)
        left, pairs = cut(2 * P), cut(2 * P)
        pos, pos_hl, pos_f = cut(TOPK).bitcast(U32), cut(2 * TOPK).bitcast(U32), cut(2 * TOPK)
        same, found = cut(2 * TOPK * TOPK), cut(2 * TOPK)
        dots, scored_gelu, weights = cut(TOPK), cut(TOPK), cut(TOPK)
        q_stat, f_stat, soft = stat[:, 0:4], stat[:, 4:8], stat[:, 8:8 + 2 * PHEADS]
        ring = [ring_mem[:, n * 2 * DM:(n + 1) * 2 * DM] for n in range(RING)]
        names = ("q_sumsq", "q_mean", "q_root", "hf_made", "hf_turned", "hf_kept", "q_made", "q_kept", "q_turned", "qt_kept", "scored",
                 "picked", "soft_in", "soft_exp", "used", "dot_made", "gelu_made", "weights_made", "diag_made", "summed",
                 "f_sumsq", "f_mean", "f_root", "out_made", "out_stored", "picks_now")
        X = {n: sem("x_" + n) for n in names}
        got = [sem(f"got{n}") for n in range(RING)]
        vector_steps, tensor_steps = sem("vector_steps"), sem("tensor_steps")
        USED0 = TOPK
        GROUPS = TOPK // GROUP
        with nc.Block() as block:
            @block.gpsimd
            def _(pool):
                with pool.Fori(0, TILES) as t:
                    pool.wait_ge(X["picked"], t * PHEADS + PHEADS)
                    pool.sem_inc(pool_steps, 1)
                    with pool.Fori(0, PHEADS) as j:
                        for half in range(2):
                            pool.wait_ge(X["used"], t * PICKS + j * TOPK + (USED0 - TOPK + 8 * half + 8))
                            pool.sem_inc(pool_steps, 1)
                            G.tensor_copy(pick_now[:, half * 8:half * 8 + 8],
                                          picks[:, ds(t * PICKS + j * TOPK + half * 8, 8)]).then_inc(X["picks_now"], 1)
                            pool.wait_ge(X["picks_now"], t * (2 * PHEADS) + j * 2 + (half + 1))
                            pool.sem_inc(pool_steps, 1)
                            for k in range(half * 8, half * 8 + 8):
                                pool.wait_ge(X["used"], t * PICKS + j * TOPK + (USED0 + k - RING + 1))
                                pool.sem_inc(pool_steps, 1)
                                G.indirect_dma_start(ring[k % RING], None, a["experts"],
                                                     bass.IndirectOffsetOnAxis(ap=pick_now[:, k:k + 1], axis=0)).then_inc(got[k % RING], 16)

            @block.sync
            def _(sp):
                with sp.Fori(0, TILES) as t:
                    sp.wait_ge(X["out_made"], t + 1)
                    sp.dma_start(out[ds(t * P, P), :], hf_t).then_inc(X["out_stored"], 16)
                sp.wait_ge(X["out_stored"], 16 * TILES)

            @block.scalar
            def _(act):
                def query(t):
                    A.activation(hf_next, h_all[:, ds(t * DM, DM)], ACT.Square, accum_out=q_stat[:, 0:1]).then_inc(X["q_sumsq"], 1)
                    act.wait_ge(X["q_mean"], t + 1)
                    A.activation(q_stat[:, 2:3], q_stat[:, 1:2], ACT.Sqrt).then_inc(X["q_root"], 1)
                    act.wait_ge(X["hf_turned"], t + 1)
                    A.activation(hf_t[:, 0:HALF], bank[0], ACT.Copy)
                    A.activation(hf_t[:, HALF:DM], bank[1], ACT.Copy).then_inc(X["hf_kept"], 1)

                def head(n):
                    act.wait_ge(X["q_made"], n + 1)
                    A.activation(q_head, bank[2][:, 0:QD], ACT.Copy).then_inc(X["q_kept"], 1)
                    act.wait_ge(X["q_turned"], n + 1)
                    A.activation(q_head_t, bank[3][:, 0:QD], ACT.Copy).then_inc(X["qt_kept"], 1)

                def softmax(t):
                    act.wait_ge(X["soft_in"], t + 1)
                    A.activation(gates, gates, ACT.Exp).then_inc(X["soft_exp"], 1)

                def experts(t, j):
                    for m in range(GROUPS):
                        of = slice(m * GROUP, (m + 1) * GROUP)
                        act.wait_ge(X["dot_made"], t * PICKS + j * TOPK + (m + 1) * GROUP)
                        A.activation(scored_gelu[:, of], dots[:, of], ACT.Gelu).then_inc(X["gelu_made"], 1)
                        act.wait_ge(X["weights_made"], t * (PHEADS * GROUPS) + j * GROUPS + (m + 1))
                        for k in range(m * GROUP, (m + 1) * GROUP):
                            act.wait_ge(X["used"], t * PICKS + j * TOPK + (USED0 + k - RING + 1))
                            A.activation(diag[k % RING], ident, ACT.Copy, scale=weights[:, k:k + 1]).then_inc(X["diag_made"], 1)

                def final(t):
                    act.wait_ge(X["summed"], t * PHEADS + PHEADS)
                    A.activation(hf_t, h_all[:, ds(t * DM, DM)], ACT.Square, accum_out=f_stat[:, 0:1]).then_inc(X["f_sumsq"], 1)
                    act.wait_ge(X["f_mean"], t + 1)
                    A.activation(f_stat[:, 2:3], f_stat[:, 1:2], ACT.Sqrt).then_inc(X["f_root"], 1)

                query(0)
                with act.Fori(0, PHEADS) as j:
                    head(j)
                with act.Fori(0, TILES - 1) as t:
                    softmax(t)
                    act.wait_ge(X["out_stored"], t * 16)
                    act.wait_ge(X["hf_made"], t + 1)
                    act.wait_ge(X["soft_in"], t + 1)
                    query(t + 1)
                    with act.Fori(0, PHEADS) as j:
                        head(t * PHEADS + (j + PHEADS))
                        experts(t, j)
                    final(t)
                softmax(TILES - 1)
                with act.Fori(0, PHEADS) as j:
                    experts(TILES - 1, j)
                act.wait_ge(X["out_stored"], 16 * (TILES - 1))
                final(TILES - 1)

            @block.vector
            def _(dve):
                def link_held(instruction):
                    vc.link(instruction)
                    V.sem_inc(vector_steps, 1)

                def query(t):
                    dve.wait_ge(X["q_sumsq"], t + 1)
                    V.tensor_scalar(q_stat[:, 1:2], q_stat[:, 0:1], 1.0 / DM, EPS, ALU.mult, ALU.add).then_inc(X["q_mean"], 1)
                    dve.wait_ge(X["q_root"], t + 1)
                    vc.link(V.reciprocal(q_stat[:, 3:4], q_stat[:, 2:3]))
                    V.scalar_tensor_tensor(hf_next, h_all[:, ds(t * DM, DM)], q_stat[:, 3:4], gain_ffn, ALU.mult, ALU.mult).then_inc(X["hf_made"], 1)

                def top16(values, indices, src, rest):
                    link_held(V.max(values[:, 0:8], src))
                    V.max_index(indices[:, 0:8], values[:, 0:8], src)
                    link_held(V.match_replace(rest, values[:, 0:8], src, LOW))
                    link_held(V.max(values[:, 8:16], rest))
                    link_held(V.max_index(indices[:, 8:16], values[:, 8:16], rest))

                def pick(piece, n, t, j):
                    if piece < 2:
                        of = slice(piece * TOPK, (piece + 1) * TOPK)
                        if piece == 0:
                            dve.wait_ge(X["scored"], n + 1)
                            V.sem_inc(vector_steps, 1)
                        top16(val[:, of], ix[:, of], bank[5][:, piece * P:(piece + 1) * P], left[:, 0:P])
                    elif piece == 2:
                        link_held(V.tensor_tensor(pairs.rearrange("p (i k) -> p i k", i=TOPK),
                                                  val[:, 0:TOPK].unsqueeze(2).to_broadcast([P, TOPK, TOPK]),
                                                  val[:, TOPK:].unsqueeze(1).to_broadcast([P, TOPK, TOPK]), ALU.add))
                        top16(val[:, 0:TOPK], pos, pairs, left)
                    else:
                        V.tensor_copy(top_val[:, ds(j * TOPK, TOPK)], val[:, 0:TOPK])
                        V.tensor_copy(ix_f, ix)
                        V.tensor_scalar(pos_hl[:, 0:TOPK], pos, 4, None, ALU.logical_shift_right)
                        vc.link(V.tensor_scalar(pos_hl[:, TOPK:], pos, TOPK - 1, None, ALU.bitwise_and))
                        vc.link(V.tensor_copy(pos_f, pos_hl))
                        three = same.rearrange("p (k i) -> p k i", i=TOPK)
                        vc.link(V.tensor_tensor(three, pos_f.unsqueeze(2).to_broadcast([P, 2 * TOPK, TOPK]),
                                                iota.unsqueeze(1).to_broadcast([P, 2 * TOPK, TOPK]), ALU.is_equal))
                        for h in range(2):
                            part = three[:, h * TOPK:(h + 1) * TOPK, :]
                            m = V.tensor_tensor(part, part, ix_f[:, h * TOPK:(h + 1) * TOPK].unsqueeze(1).to_broadcast([P, TOPK, TOPK]), ALU.mult)
                        vc.link(m)
                        vc.link(V.tensor_reduce(found, three, AX.X, ALU.add))
                        V.scalar_tensor_tensor(picks[:, ds(t * PICKS + j * TOPK, TOPK)], found[:, 0:TOPK], float(NKEYS),
                                               found[:, TOPK:], ALU.mult, ALU.add).then_inc(X["picked"], 1)
                        dve.wait_ge(X["picked"], n + 1)

                def softmax(t):
                    shape = [P, PHEADS, TOPK]
                    vals, g = (ap.rearrange("p (h k) -> p h k", h=PHEADS) for ap in (top_val, gates))
                    V.tensor_copy(hf_now, hf_next)
                    V.tensor_tensor(g, vals, vals[:, :, 0:1].to_broadcast(shape), ALU.subtract).then_inc(X["soft_in"], 1)
                    dve.wait_ge(X["soft_exp"], t + 1)
                    vc.link(V.tensor_reduce(soft[:, 0:PHEADS], g, AX.X, ALU.add))
                    vc.link(V.reciprocal(soft[:, PHEADS:], soft[:, 0:PHEADS]))
                    vc.link(V.tensor_tensor(g, g, soft[:, PHEADS:].unsqueeze(2).to_broadcast(shape), ALU.mult))

                def experts(t, j, picking):
                    for m in range(GROUPS):
                        for k in range(m * GROUP, (m + 1) * GROUP):
                            dve.wait_ge(got[k % RING], t * (PICKS * 16 // RING) + j * (TOPK * 16 // RING) + 16 * (k // RING + 1))
                            row = ring[k % RING][:, 0:DM]
                            V.tensor_tensor_reduce(out=row, in0=row, in1=hf_now, scale=1.0, scalar=0.0, op0=ALU.mult, op1=ALU.add,
                                                   accum_out=dots[:, k:k + 1]).then_inc(X["dot_made"], 1)
                        if picking:
                            pick(m, t * PHEADS + (j + PHEADS), t + 1, j)
                        of = slice(m * GROUP, (m + 1) * GROUP)
                        dve.wait_ge(X["gelu_made"], t * (PHEADS * GROUPS) + j * GROUPS + (m + 1))
                        V.tensor_tensor(weights[:, of], scored_gelu[:, of], gates[:, ds(j * TOPK + m * GROUP, GROUP)],
                                        ALU.mult).then_inc(X["weights_made"], 1)
                    dve.wait_ge(X["used"], t * PICKS + j * TOPK + (USED0 + TOPK))
                    for half in range(2):
                        at = h_all[:, ds(t * DM + half * HALF, HALF)]
                        m = V.tensor_tensor(at, bank[6 + half], at, ALU.add)
                    m.then_inc(X["summed"], 1)
                    dve.wait_ge(X["summed"], t * PHEADS + (j + 1))

                def final(t):
                    dve.wait_ge(X["f_sumsq"], t + 1)
                    V.tensor_scalar(f_stat[:, 1:2], f_stat[:, 0:1], 1.0 / DM, EPS, ALU.mult, ALU.add).then_inc(X["f_mean"], 1)
                    dve.wait_ge(X["f_root"], t + 1)
                    vc.link(V.reciprocal(f_stat[:, 3:4], f_stat[:, 2:3]))
                    V.scalar_tensor_tensor(hf_t, h_all[:, ds(t * DM, DM)], f_stat[:, 3:4], gain_fin, ALU.mult, ALU.mult).then_inc(X["out_made"], 1)

                dve.wait_ge(keys_in, 48)
                V.memset(dots, 0.0).then_inc(X["used"], USED0)
                query(0)
                with vc.loop(PHEADS, 18) as j:
                    for piece in range(4):
                        pick(piece, j + 0, 0, j)
                with vc.loop(TILES - 1, PHEADS * 18 + 5) as t:
                    softmax(t)
                    query(t + 1)
                    with vc.loop(PHEADS, 18) as j:
                        experts(t, j, True)
                    final(t)
                softmax(TILES - 1)
                with dve.Fori(0, PHEADS) as j:
                    experts(TILES - 1, j, False)
                final(TILES - 1)

            @block.tensor
            def _(pe):
                def query(t):
                    pe.wait_ge(X["hf_made"], t + 1)
                    for d in range(DB):
                        m = PE.transpose(bank[d // 4][:, (d % 4) * P:(d % 4 + 1) * P], hf_next[:, d * P:(d + 1) * P], ident)
                    m.then_inc(X["hf_turned"], 1)
                    pe.wait_ge(X["hf_kept"], t + 1)
                    pe.sem_inc(tensor_steps, 1)

                def head(n, j):
                    pe.wait_ge(X["q_kept"], n)
                    for d in range(DB):
                        m = PE.matmul(bank[2][:, 0:QD], hf_t[:, d * P:(d + 1) * P],
                                      w_query[:, ds(j * QD + d * (PHEADS * QD), QD)], start=(d == 0), stop=(d == DB - 1))
                    m.then_inc(X["q_made"], 1)
                    pe.wait_ge(X["q_kept"], n + 1)
                    for h in range(2):
                        m = PE.transpose(bank[3][:, h * P:(h + 1) * P], q_head[:, h * P:(h + 1) * P], ident)
                    m.then_inc(X["q_turned"], 1)
                    pe.wait_ge(X["qt_kept"], n + 1)
                    pe.wait_ge(X["picked"], n)
                    for h in range(2):
                        m = PE.matmul(bank[5][:, h * P:(h + 1) * P], q_head_t[:, h * P:(h + 1) * P],
                                      sub_keys[:, ds(j * QD + h * P, P)], start=True, stop=True)
                    m.then_inc(X["scored"], 1)

                def experts(t, j):
                    pe.wait_ge(X["summed"], t * PHEADS + j)
                    for k in range(TOPK):
                        pe.wait_ge(X["diag_made"], t * PICKS + j * TOPK + (k + 1))
                        for half in range(2):
                            m = PE.matmul(bank[6 + half], diag[k % RING], ring[k % RING][:, DM + half * HALF:DM + (half + 1) * HALF],
                                          start=(k == 0), stop=(k == TOPK - 1))
                        m.then_inc(X["used"], 1)

                pe.wait_ge(w_query_in, 16)
                pe.wait_ge(keys_in, 48)
                query(0)
                with pe.Fori(0, PHEADS) as j:
                    head(j + 0, j)
                with pe.Fori(0, TILES - 1) as t:
                    query(t + 1)
                    with pe.Fori(0, PHEADS) as j:
                        head(t * PHEADS + (j + PHEADS), j)
                        experts(t, j)
                with pe.Fori(0, PHEADS) as j:
                    experts(TILES - 1, j)
    return nc


def kernel(x, norm_mix_gain, w_in, conv_w, a_log, dt_bias, gdn_out_gain, w_pool, b_pool, pool_scale, w_out,
           norm_ffn_gain, peer_w_query, peer_sub_keys_1, peer_sub_keys_2, peer_expert_u, peer_expert_v,
           norm_final_gain):
    import concourse.bacc as bacc
    from concourse.bass_utils import run_bass_kernel_spmd

    data = layout(x, norm_mix_gain, w_in, conv_w, a_log, dt_bias, gdn_out_gain, w_pool, b_pool, pool_scale, w_out,
                  norm_ffn_gain, peer_w_query, peer_sub_keys_1, peer_sub_keys_2, peer_expert_u, peer_expert_v,
                  norm_final_gain)
    nc = bacc.Bacc("TRN2", target_bir_lowering=False, num_devices=1)
    ins = {n: nc.dram_tensor("in_" + n, v.shape, mybir.dt.from_np(v.dtype), kind="ExternalInput").ap() for n, v in data.items()}
    out = nc.dram_tensor("out", (SEQ, DM), mybir.dt.float32, kind="ExternalOutput").ap()
    build(nc, ins, out)
    r = run_bass_kernel_spmd(nc, [{"in_" + n: v for n, v in data.items()}], core_ids=[0])
    return r.results[0]["out"].reshape(1, SEQ, DM)


def layout(x, norm_mix_gain, w_in, conv_w, a_log, dt_bias, gdn_out_gain, w_pool, b_pool, pool_scale, w_out,
           norm_ffn_gain, peer_w_query, peer_sub_keys_1, peer_sub_keys_2, peer_expert_u, peer_expert_v,
           norm_final_gain):
    def rows(w):
        w = np.asarray(w)
        return w.reshape(-1, P, w.shape[1]).transpose(1, 0, 2).reshape(P, -1)

    w_in = np.asarray(w_in)[0]
    n_mixed = HALF + 3 * HALF
    wc = w_in[:, :n_mixed].reshape(DB, P, n_mixed // P, P).transpose(2, 1, 0, 3).reshape(n_mixed // P, P, DM)
    taps = np.asarray(conv_w)[0].reshape(TAPS, 12, P).transpose(2, 1, 0).reshape(P, 12 * TAPS)
    keys = np.stack([np.asarray(peer_sub_keys_1)[0], np.asarray(peer_sub_keys_2)[0]], axis=1)
    data = {
        "x": np.asarray(x)[0],
        "constants": constants(),
        "gain_mix": np.asarray(norm_mix_gain)[0],
        "gain_ffn": np.asarray(norm_ffn_gain)[0],
        "gain_fin": np.asarray(norm_final_gain),
        "out_gain": np.asarray(gdn_out_gain)[0],
        "wc": wc,
        "wz": rows(w_in[:, n_mixed:n_mixed + HALF]),
        "wab": rows(w_in[:, n_mixed + HALF:]),
        "per_channel": np.concatenate([taps, np.asarray(b_pool)[0].T, np.asarray(pool_scale)[0].reshape(4, P).T], axis=1),
        "per_head": np.concatenate([np.asarray(a_log)[0], np.asarray(dt_bias)[0]]),
        "w_pool": np.asarray(w_pool)[0].transpose(1, 0, 2).reshape(P, 4 * P),
        "w_out": rows(np.asarray(w_out)[0]),
        "w_query": rows(np.asarray(peer_w_query)[0]),
        "sub_keys": keys.transpose(3, 0, 1, 2).reshape(P, 2 * PHEADS * NKEYS),
        "experts": np.concatenate([np.asarray(peer_expert_u)[0], np.asarray(peer_expert_v)[0]], axis=1),
    }
    return {n: np.ascontiguousarray(v) for n, v in data.items()}
```

```python
from contextlib import ExitStack, contextmanager

import numpy as np

import concourse.bass as bass
from concourse import mybir

P = 128
SEQ, DM = 1024, 1024
TILES = SEQ // P
DB = DM // P
CHUNK = 64
HALF = 512
HEADS = 4
HD = 128
POOL_WINDOWS = (2, 4, 8, 16)
PAD = 16
TAPS = 4
EPS = 1e-6
PHEADS, NKEYS, TOPK = 8, 128, 16
QD = 2 * P
PICKS = PHEADS * TOPK
LEVELS = (2, 4, 8, 16, 32)
RING = 8
GROUP = 4
LOW = -3.0e38


class Chain:

    def __init__(self, engine, sem):
        self.engine, self.sem, self.base, self.n = engine, sem, 0, 0

    def link(self, instruction):
        self.n += 1
        instruction.then_inc(self.sem, 1)
        self.engine.wait_ge(self.sem, self.base + self.n)

    @contextmanager
    def loop(self, first, end, links):
        base, n = self.base, self.n
        with self.engine.Fori(first, end) as i:
            if links:
                self.base, self.n = i * links + (base + n - first * links), 0
            yield i
            assert self.n - (0 if links else n) == links, f"the body makes {self.n} links"
        self.base, self.n = base, n + (end - first) * links


class Cut:

    def __init__(self, ap):
        self.ap, self.at = ap, 0

    def __call__(self, cols):
        self.at += cols
        assert self.at <= self.ap.shape[1], (self.at, self.ap.shape)
        return self.ap[:, self.at - cols:self.at]


def constants():
    j, i = np.arange(P)[:, None], np.arange(P)[None, :]
    same = (j // CHUNK) == (i // CHUNK)
    cols = [j == i, np.broadcast_to(np.arange(TOPK), (P, TOPK)),
            np.ones((P, P)), same & (j <= i), same & (j > i)]
    for s in (1,) + LEVELS:
        cols.append((j // (2 * s) == i // (2 * s)) & (j % (2 * s) < s) & (i % (2 * s) >= s))
    for w in POOL_WINDOWS:
        cols.append(np.broadcast_to(1.0 / np.minimum(np.arange(PAD) + 1, w), (P, PAD)))
    return np.concatenate([c.astype(np.float32) for c in cols], axis=1)


N_KEPT = P + TOPK
N_MASKS = (3 + 1 + len(LEVELS)) * P + len(POOL_WINDOWS) * PAD


def build(nc, a, out):
    F32, I32, U32 = mybir.dt.float32, mybir.dt.int32, mybir.dt.uint32
    ALU, ACT, AX = mybir.AluOpType, mybir.ActivationFunctionType, mybir.AxisListType
    PE, V, A, G = nc.tensor, nc.vector, nc.scalar, nc.gpsimd
    ds = bass.ds
    top = ExitStack()

    def sb(name, cols, dtype=F32):
        return top.enter_context(nc.sbuf_tensor(name, [P, cols], dtype))[:, :]

    def sem(name):
        return top.enter_context(nc.semaphore(name))

    def per_head(ap):
        return ap.rearrange("p (h c) -> p h c", h=HEADS)

    def over_heads(ap):
        return ap.unsqueeze(1).to_broadcast([P, HEADS, P])

    def over_cols(ap, cols=P):
        return ap.unsqueeze(2).to_broadcast([ap.shape[0], ap.shape[1], cols])

    with top:
        bank = [top.enter_context(nc.psum_tensor(f"bank{n}", [P, HALF], F32))[:, :] for n in range(8)]
        pool_steps = sem("pool_steps")
        vc, ac = Chain(V, sem("vector_chain")), Chain(A, sem("scalar_chain"))

        kept = sb("kept", N_KEPT)
        ident, iota = kept[:, 0:P], kept[:, P:P + TOPK]
        h_all = sb("h_all", TILES * DM)
        gain_ffn = sb("gain_ffn", DM)
        gain_fin = sb("gain_fin", DM)
        stat = sb("stat", 32)
        ffn_rstd = sb("ffn_rstd", TILES)
        eps_col = sb("eps_col", 2)
        late = sb("late", 2 * 8 * DM)
        late_spare = late[:, 12 * SEQ:]
        ring_mem = sb("ring_mem", RING * 2 * DM)
        work = sb("work", 9900)

        w_score = late
        qkv_t = late[:, 0:12 * SEQ]
        z_all = ring_mem[:, 0:TILES * HALF]
        o_all = ring_mem[:, TILES * HALF:2 * TILES * HALF]
        hn_t = ring_mem[:, 2 * TILES * HALF:2 * TILES * HALF + DB * SEQ]

        mix = Cut(work)
        masks = mix(N_MASKS)
        ones, causal, after = (masks[:, n * P:(n + 1) * P] for n in range(3))
        level_mask = [masks[:, (3 + n) * P:(4 + n) * P] for n in range(6)]
        inv_count = masks[:, 9 * P:]
        small = mix(64)
        conv_w, b_pool, pool_scale = small[:, 0:48], small[:, 48:52], small[:, 52:56]
        a_log, dt_bias = small[:, 56:60], small[:, 60:64]
        out_gain = mix(HD)
        ab_all = mix(TILES * 8)
        pool_t = mix(4 * SEQ)

        early = Cut(late)
        wz, wab, gain_mix, hn, hn_tile, junk = early(DB * HALF), early(DB * 8), early(DM), early(DM), early(DM), early(DM)
        x_in, const_in, wz_in, small_in, gains_in = (sem(n) for n in ("x_in", "const_in", "wz_in", "small_in", "gains_in"))
        sq_made, ms_made, root_made, rstd_made = (sem(n) for n in ("sumsq_made", "mean_made", "root_made", "rstd_made"))
        hn_made, turned, tile_kept, z_made, z_kept, hn_kept = (
            sem(n) for n in ("hn_made", "hn_turned", "hn_tile_kept", "z_made", "z_kept", "hn_kept"))
        with nc.Block() as block:
            @block.sync
            def _(sp):
                sp.dma_start(h_all.rearrange("p (t d) -> p t d", t=TILES),
                             a["x"].rearrange("(t p) d -> p t d", p=P)).then_inc(x_in, 16)
                sp.dma_start(kept, a["constants"][:, 0:N_KEPT]).then_inc(const_in, 16)
                sp.dma_start(gain_mix, a["gain_mix"].partition_broadcast(P)).then_inc(const_in, 16)
                sp.dma_start(wz, a["wz"]).then_inc(wz_in, 16)
                sp.dma_start(wab, a["wab"]).then_inc(wz_in, 16)
                sp.dma_start(masks, a["constants"][:, N_KEPT:]).then_inc(small_in, 16)
                sp.dma_start(small[:, 0:56], a["per_channel"]).then_inc(small_in, 16)
                sp.dma_start(small[:, 56:64], a["per_head"].partition_broadcast(P)).then_inc(small_in, 16)
                sp.dma_start(out_gain, a["out_gain"].partition_broadcast(P)).then_inc(small_in, 16)
                sp.dma_start(gain_ffn, a["gain_ffn"].partition_broadcast(P)).then_inc(gains_in, 16)
                sp.dma_start(gain_fin, a["gain_fin"].partition_broadcast(P)).then_inc(gains_in, 16)

            @block.scalar
            def _(act):
                act.wait_ge(x_in, 16)
                with act.Fori(0, TILES) as t:
                    A.activation(junk, h_all[:, ds(t * DM, DM)], ACT.Square,
                                 accum_out=stat[:, ds(t, 1)]).then_inc(sq_made, 1)
                    act.wait_ge(sq_made, t + 1)
                act.wait_ge(ms_made, 1)
                A.activation(stat[:, 16:24], stat[:, 8:16], ACT.Sqrt).then_inc(root_made, 1)
                with act.Fori(0, TILES) as t:
                    act.wait_ge(turned, t + 1)
                    act.wait_ge(z_made, t)
                    act.wait_ge(hn_kept, t)
                    A.activation(hn_tile[:, 0:HALF], bank[0], ACT.Copy)
                    A.activation(hn_tile[:, HALF:DM], bank[1], ACT.Copy).then_inc(tile_kept, 1)
                    act.wait_ge(z_made, t + 1)
                    A.activation(z_all[:, ds(t * HALF, HALF)], bank[2], ACT.Copy)
                    A.activation(ab_all[:, ds(t * 8, 8)], bank[3][:, 0:8], ACT.Copy).then_inc(z_kept, 1)

            @block.vector
            def _(dve):
                V.memset(eps_col[:, 0:1], EPS * HD)
                V.memset(eps_col[:, 1:2], EPS)
                dve.wait_ge(sq_made, TILES)
                V.tensor_scalar(stat[:, 8:16], stat[:, 0:8], 1.0 / DM, EPS, ALU.mult, ALU.add).then_inc(ms_made, 1)
                dve.wait_ge(root_made, 1)
                V.reciprocal(stat[:, 24:32], stat[:, 16:24]).then_inc(rstd_made, 1)
                dve.wait_ge(rstd_made, 1)
                dve.wait_ge(const_in, 32)
                with dve.Fori(0, TILES) as t:
                    dve.wait_ge(turned, t)
                    V.scalar_tensor_tensor(hn, h_all[:, ds(t * DM, DM)], stat[:, ds(t + 24, 1)],
                                           gain_mix, ALU.mult, ALU.mult).then_inc(hn_made, 1)

            @block.tensor
            def _(pe):
                pe.wait_ge(const_in, 32)
                pe.wait_ge(wz_in, 32)
                with pe.Fori(0, TILES) as t:
                    pe.wait_ge(hn_made, t + 1)
                    pe.wait_ge(tile_kept, t)
                    for d in range(DB):
                        m = PE.transpose(bank[d // 4][:, (d % 4) * P:(d % 4 + 1) * P], hn[:, d * P:(d + 1) * P], ident)
                    m.then_inc(turned, 1)
                    pe.wait_ge(tile_kept, t + 1)
                    pe.wait_ge(z_kept, t)
                    for d in range(DB):
                        PE.matmul(bank[2], hn_tile[:, d * P:(d + 1) * P], wz[:, d * HALF:(d + 1) * HALF],
                                  start=(d == 0), stop=(d == DB - 1))
                    for d in range(DB):
                        m = PE.matmul(bank[3][:, 0:8], hn_tile[:, d * P:(d + 1) * P], wab[:, d * 8:(d + 1) * 8],
                                      start=(d == 0), stop=(d == DB - 1))
                    m.then_inc(z_made, 1)

            @block.gpsimd
            def _(pool):
                with pool.Fori(0, TILES) as t:
                    pool.wait_ge(tile_kept, t + 1)
                    pool.sem_inc(pool_steps, 1)
                    G.tensor_copy(hn_t.rearrange("p (d s) -> p d s", d=DB)[:, :, ds(t * P, P)],
                                  hn_tile.rearrange("p (d s) -> p d s", d=DB)).then_inc(hn_kept, 1)

        wc = [late[:, 12 * SEQ + n * DM:12 * SEQ + (n + 1) * DM] for n in range(4)]
        spare, rest = Cut(o_all), Cut(work[:, mix.at:])
        raw = [spare(PAD + SEQ), spare(PAD + SEQ)]
        y = [spare(PAD + SEQ), rest(PAD + SEQ)]
        diff = rest(SEQ)
        w_pool = spare(4 * P)
        wc_in = [sem(f"wc_in{n}") for n in range(4)]
        pool_w_in, proj_made, raw_kept, sums_made, silu_made, pooled, pool_kept, pads_made = (
            sem(n) for n in ("pool_w_in", "proj_made", "raw_kept", "sums_made", "silu_made", "pooled", "pool_kept", "pads_made"))
        with nc.Block() as block:
            @block.sync
            def _(sp):
                for s in range(4):
                    sp.dma_start(wc[s], a["wc"][s, :, :]).then_inc(wc_in[s], 16)
                sp.dma_start(w_pool, a["w_pool"]).then_inc(pool_w_in, 16)
                with sp.Fori(0, 3) as i:
                    for s in range(4):
                        sp.wait_ge(proj_made, i * 8 + (2 * s + 2))
                        sp.dma_start(wc[s], a["wc"][ds(i * 4 + (4 + s), 1), :, :].rearrange("a p c -> p (a c)")).then_inc(wc_in[s], 16)

            @block.tensor
            def _(pe):
                def project(s, loaded, before):
                    pe.wait_ge(wc_in[s], loaded)
                    for half in range(2):
                        if before is not None:
                            pe.wait_ge(raw_kept, before + half)
                        for d in range(DB):
                            m = PE.matmul(bank[2 * (s % 2) + half], wc[s][:, d * P:(d + 1) * P],
                                          hn_t[:, d * SEQ + half * HALF:d * SEQ + (half + 1) * HALF],
                                          start=(d == 0), stop=(d == DB - 1))
                        m.then_inc(proj_made, 1)

                def pool_product(g):
                    pe.wait_ge(sums_made, g + 1)
                    if g > 0:
                        pe.wait_ge(pool_kept, 2 * g)
                    for half in range(2):
                        PE.matmul(bank[4 + half], w_pool[:, g * P:(g + 1) * P], diff[:, half * HALF:(half + 1) * HALF],
                                  start=True, stop=True).then_inc(pooled, 1)

                project(0, 16, None)
                project(1, 16, None)
                pe.wait_ge(pool_w_in, 16)
                pool_product(0)
                project(2, 16, 1)
                pool_product(1)
                project(3, 16, 3)
                pool_product(2)
                pool_product(3)
                with pe.Fori(0, 3) as i:
                    for s in range(4):
                        project(s, i * 16 + 32, i * 8 + (2 * s + 5))

            @block.scalar
            def _(act):
                def keep_raw(s, made, read):
                    for half in range(2):
                        act.wait_ge(proj_made, made + half)
                        if half == 0 and read is not None:
                            act.wait_ge(sums_made, read)
                        A.activation(raw[s % 2][:, PAD + half * HALF:PAD + (half + 1) * HALF],
                                     bank[2 * (s % 2) + half], ACT.Copy).then_inc(raw_kept, 1)

                act.wait_ge(pads_made, 1)
                for s in range(4):
                    keep_raw(s, 2 * s + 1, s - 1 if s >= 2 else None)
                with act.Fori(0, 3) as i:
                    for s in range(4):
                        keep_raw(s, i * 8 + (2 * s + 9), i * 4 + (s + 3))
                        act.wait_ge(sums_made, i * 4 + (s + 5))
                        A.activation(qkv_t[:, ds(i * (4 * SEQ) + s * SEQ, SEQ)], y[s % 2][:, PAD:],
                                     ACT.Silu).then_inc(silu_made, 1)

            @block.vector
            def _(dve):
                def pool_out(g):
                    for half in range(2):
                        dve.wait_ge(pooled, 2 * g + half + 1)
                        V.tensor_scalar(pool_t[:, g * SEQ + half * HALF:g * SEQ + (half + 1) * HALF], bank[4 + half],
                                        b_pool[:, g:g + 1], pool_scale[:, g:g + 1], ALU.add, ALU.mult).then_inc(pool_kept, 1)

                dve.wait_ge(pads_made, 1)
                dve.wait_ge(small_in, 64)
                for g, window in enumerate(POOL_WINDOWS):
                    dve.wait_ge(raw_kept, 2 * g + 2)
                    src, reach, n = raw[g % 2], 1, 0
                    while reach < window:
                        dst = y[n % 2]
                        vc.link(V.tensor_tensor(dst[:, PAD:], src[:, PAD:], src[:, PAD - reach:PAD + SEQ - reach], ALU.add))
                        src, reach, n = dst, 2 * reach, n + 1
                    if g > 0:
                        dve.wait_ge(pooled, 2 * g)
                    vc.link(V.scalar_tensor_tensor(diff, src[:, PAD:], 1.0 / window, raw[g % 2][:, PAD:], ALU.mult, ALU.subtract))
                    vc.link(V.tensor_tensor(diff[:, 0:PAD], src[:, PAD:2 * PAD], inv_count[:, g * PAD:(g + 1) * PAD], ALU.mult))
                    V.tensor_tensor(diff[:, 0:PAD], diff[:, 0:PAD], raw[g % 2][:, PAD:2 * PAD], ALU.subtract).then_inc(sums_made, 1)
                    dve.wait_ge(sums_made, g + 1)
                    if g > 0:
                        pool_out(g - 1)
                pool_out(3)
                with vc.loop(0, 3, 4 * (TAPS - 1)) as i:
                    for s in range(4):
                        dve.wait_ge(raw_kept, i * 8 + (2 * s + 10))
                        dst = y[s % 2][:, PAD:]
                        taps = [small[:, ds(i * 16 + (4 * s + k), 1)] for k in range(TAPS)]
                        dve.wait_ge(silu_made, i * 4 + max(s - 1, 0))
                        vc.link(V.tensor_scalar(dst, raw[s % 2][:, PAD:], taps[TAPS - 1], None, ALU.mult))
                        for k in range(1, TAPS):
                            m = V.scalar_tensor_tensor(dst, raw[s % 2][:, PAD - k:PAD + SEQ - k], taps[TAPS - 1 - k], dst, ALU.mult, ALU.add)
                            if k < TAPS - 1:
                                vc.link(m)
                            else:
                                m.then_inc(sums_made, 1)
                                dve.wait_ge(sums_made, i * 4 + (s + 5))

            @block.gpsimd
            def _(pool):
                for buf in (raw[0], raw[1], y[0]):
                    G.memset(buf[:, 0:PAD], 0.0)
                G.memset(y[1][:, 0:PAD], 0.0).then_inc(pads_made, 1)

        cut = Cut(hn_t)
        square = [cut(SEQ), cut(SEQ)]
        root = [cut(SEQ), cut(SEQ)]
        square_made, square_sum, norm_root, normed = (sem(n) for n in ("square_made", "square_sum", "norm_root", "qk_normed"))
        with nc.Block() as block:
            @block.scalar
            def _(act):
                for q_or_k, scale in enumerate((float(HD), 1.0)):
                    with act.Fori(0, HEADS // 2) as i:
                        for s in range(2):
                            before = i * 2 + (4 * q_or_k + s)
                            src = qkv_t[:, ds(i * (2 * SEQ) + (4 * q_or_k + s) * SEQ, SEQ)]
                            A.activation(square[s], src, ACT.Square).then_inc(square_made, 1)
                            act.wait_ge(square_sum, before + 1)
                            act.wait_ge(normed, i * 2 + (4 * q_or_k))
                            for half in range(2):
                                m = A.activation(root[s][:, half * HALF:(half + 1) * HALF], bank[2 * s + half], ACT.Sqrt,
                                                 scale=scale, bias=eps_col[:, q_or_k:q_or_k + 1])
                            m.then_inc(norm_root, 1)

            @block.tensor
            def _(pe):
                with pe.Fori(0, HEADS) as i:
                    for s in range(2):
                        pe.wait_ge(square_made, i * 2 + (s + 1))
                        pe.wait_ge(norm_root, i * 2 + 0)
                        for half in range(2):
                            m = PE.matmul(bank[2 * s + half], ones, square[s][:, half * HALF:(half + 1) * HALF], start=True, stop=True)
                        m.then_inc(square_sum, 1)

            @block.vector
            def _(dve):
                with vc.loop(0, HEADS, 2) as i:
                    for s in range(2):
                        dve.wait_ge(norm_root, i * 2 + (s + 1))
                        vc.link(V.reciprocal(root[s], root[s]))
                        at = qkv_t[:, ds(i * (2 * SEQ) + s * SEQ, SEQ)]
                        V.tensor_tensor(at, at, root[s], ALU.mult).then_inc(normed, 1)

        TH = TILES * HEADS
        cut = Cut(work[:, mix.at:])
        log_dec, log_sum, beta, beta_dec, dec_end, sp_a, sp_b, sp_c = (cut(TH) for _ in range(8))
        exp_sum = sp_a
        b_raw = ab_all.rearrange("p (t c) -> p t c", t=TILES)[:, :, 0:HEADS]
        a_raw = ab_all.rearrange("p (t c) -> p t c", t=TILES)[:, :, HEADS:2 * HEADS]

        def by_tile(ap):
            return ap.rearrange("p (t h) -> p t h", t=TILES)

        def over_tiles(ap):
            return ap.unsqueeze(1).to_broadcast([P, TILES, HEADS])

        soft_in, soft_e, soft_l, dec_made, sums_done, exps_done = (
            sem(n) for n in ("softplus_in", "softplus_exp", "softplus_log", "log_decay_made", "decay_sums_made", "decay_exps_made"))
        with nc.Block() as block:
            @block.vector
            def _(dve):
                vc.link(V.tensor_tensor(by_tile(sp_a), a_raw, over_tiles(dt_bias), ALU.add))
                vc.link(V.tensor_scalar(sp_b, sp_a, -1.0, None, ALU.mult))
                V.tensor_tensor(sp_b, sp_b, sp_a, ALU.min).then_inc(soft_in, 1)
                dve.wait_ge(soft_e, 3)
                vc.link(V.tensor_scalar(beta, beta, 1.0, None, ALU.add))
                vc.link(V.reciprocal(beta, beta))
                dve.wait_ge(soft_l, 1)
                vc.link(V.scalar_tensor_tensor(sp_c, sp_a, 0.0, sp_c, ALU.max, ALU.add))
                V.scalar_tensor_tensor(by_tile(log_dec), by_tile(sp_c), -1.0, over_tiles(stat[:, 0:HEADS]), ALU.mult, ALU.mult).then_inc(dec_made, 1)
                dve.wait_ge(exps_done, 1)
                vc.link(V.tensor_copy(log_sum, bank[0][:, 0:TH]))
                vc.link(V.tensor_tensor(beta_dec, beta, exp_sum, ALU.mult))

            @block.scalar
            def _(act):
                A.activation(stat[:, 0:HEADS], a_log, ACT.Exp).then_inc(soft_e, 1)
                A.activation(by_tile(beta), b_raw, ACT.Exp, scale=-1.0).then_inc(soft_e, 1)
                act.wait_ge(soft_in, 1)
                A.activation(sp_b, sp_b, ACT.Exp).then_inc(soft_e, 1)
                act.wait_ge(soft_e, 3)
                A.activation(sp_c, sp_b, ACT.Ln, bias=1.0).then_inc(soft_l, 1)
                act.wait_ge(sums_done, 1)
                A.activation(exp_sum, bank[0][:, 0:TH], ACT.Exp)
                A.activation(dec_end, bank[0][:, TH:2 * TH], ACT.Exp).then_inc(exps_done, 1)

            @block.tensor
            def _(pe):
                pe.wait_ge(dec_made, 1)
                PE.matmul(bank[0][:, 0:TH], causal, log_dec, start=True, stop=True)
                PE.matmul(bank[0][:, TH:2 * TH], after, log_dec, start=True, stop=True).then_inc(sums_done, 1)

        pieces = [hn_t[:, n * HALF:(n + 1) * HALF] for n in range(16)]
        pieces += [late[:, 12 * SEQ + n * HALF:12 * SEQ + (n + 1) * HALF] for n in range(8)]
        pieces += [cut(HALF) for _ in range(3)]
        (sum_rhs, beta_rhs, k_tile, v_tile, dec, row_dec, solve, scores, q_first, q_second, v_beta, k_beta, k_first, k_second,
         inv, inv_t, prod, u_tile, w_tile, v_new, state, middle) = pieces[:22]
        lower = pieces[22:27]
        q_all, k_all, v_all = (qkv_t[:, n * 4 * SEQ:(n + 1) * 4 * SEQ].rearrange("p (h s) -> p h s", h=HEADS) for n in range(3))
        names = ("zeroed", "kv_kept", "sum_rhs_made", "beta_rhs_made", "rows_made", "kk_made", "turned_kv", "diff_made", "rows_exp",
                 "solve_made", "lower_made", "inv_t_made", "inv_turned", "inv_made", "prod_made", "prod_kept", "corr_made", "level_done",
                 "tokens_made", "uw_made", "uw_kept", "ws_made", "v_new_made", "gain_made", "state_made", "o_made", "o_kept")
        S = {n: sem("d_" + n) for n in names}
        NL = len(LEVELS)
        with nc.Block() as block:
            @block.gpsimd
            def _(pool):
                for buf in (state, v_new, q_first, q_second, k_first):
                    G.memset(buf, 0.0)
                G.memset(k_second, 0.0).then_inc(S["zeroed"], 1)
                with pool.Fori(0, TILES) as t:
                    pool.wait_ge(S["rows_made"], t)
                    pool.sem_inc(pool_steps, 1)
                    G.tensor_tensor(per_head(beta_rhs), over_heads(ident), over_cols(beta[:, ds(t * HEADS, HEADS)]), ALU.mult).then_inc(S["beta_rhs_made"], 1)
                    pool.wait_ge(S["solve_made"], t + 1)
                    pool.wait_ge(S["level_done"], t * NL)
                    for n in range(NL):
                        G.tensor_tensor(per_head(lower[n]), per_head(solve), over_heads(level_mask[n + 1]), ALU.mult).then_inc(S["lower_made"], 1)

            @block.scalar
            def _(act):
                with act.Fori(0, TILES) as t:
                    act.wait_ge(S["turned_kv"], t)
                    A.activation(per_head(k_tile), k_all[:, :, ds(t * P, P)], ACT.Copy)
                    A.activation(per_head(v_tile), v_all[:, :, ds(t * P, P)], ACT.Copy).then_inc(S["kv_kept"], 1)
                    act.wait_ge(S["diff_made"], t + 1)
                    act.wait_ge(S["state_made"], t * 2)
                    A.activation(row_dec, bank[0], ACT.Exp).then_inc(S["rows_exp"], 1)
                    A.activation(dec, dec, ACT.Exp).then_inc(S["rows_exp"], 1)
                    act.wait_ge(S["inv_turned"], t + 1)
                    A.activation(inv, bank[6], ACT.Copy).then_inc(S["inv_made"], 1)
                    for n in range(NL):
                        act.wait_ge(S["prod_made"], t * NL + n + 1)
                        A.activation(prod, bank[6], ACT.Copy).then_inc(S["prod_kept"], 1)
                    act.wait_ge(S["uw_made"], t + 1)
                    A.activation(u_tile, bank[2], ACT.Copy)
                    A.activation(w_tile, bank[3], ACT.Copy).then_inc(S["uw_kept"], 1)
                    act.wait_ge(S["o_made"], t + 1)
                    A.activation(o_all[:, ds(t * HALF, HALF)], bank[7], ACT.Copy).then_inc(S["o_kept"], 1)

            @block.vector
            def _(dve):
                dve.wait_ge(S["zeroed"], 1)
                with vc.loop(0, TILES, 5) as t:
                    four = ds(t * HEADS, HEADS)
                    dve.wait_ge(S["rows_made"], t)
                    V.tensor_tensor(per_head(sum_rhs), over_heads(causal), over_cols(log_dec[:, four]), ALU.mult).then_inc(S["sum_rhs_made"], 1)
                    dve.wait_ge(S["rows_made"], t + 1)
                    vc.link(V.tensor_tensor(per_head(dec), per_head(bank[0]), over_cols(log_sum[:, four]), ALU.subtract))
                    V.tensor_tensor(per_head(dec), per_head(dec), over_heads(causal), ALU.mult).then_inc(S["diff_made"], 1)
                    dve.wait_ge(S["rows_exp"], t * 2 + 2)
                    vc.link(V.tensor_tensor(per_head(dec), per_head(dec), over_heads(causal), ALU.mult))
                    dve.wait_ge(S["kk_made"], t + 1)
                    dve.wait_ge(S["lower_made"], t * NL)
                    dve.wait_ge(S["o_made"], t)
                    vc.link(V.tensor_tensor(solve, bank[2], dec, ALU.mult))
                    V.tensor_tensor(solve, solve, bank[1], ALU.mult).then_inc(S["solve_made"], 1)
                    vc.link(V.tensor_tensor(scores, bank[3], dec, ALU.mult))
                    dve.wait_ge(S["solve_made"], t + 1)
                    vc.link(V.tensor_tensor(per_head(inv_t), per_head(solve), over_heads(level_mask[0]), ALU.mult))
                    V.tensor_tensor(per_head(inv_t), over_heads(ident), per_head(inv_t), ALU.subtract).then_inc(S["inv_t_made"], 1)
                    dve.wait_ge(S["turned_kv"], t + 1)
                    V.tensor_tensor(per_head(v_beta), per_head(bank[5]), over_cols(beta[:, four]), ALU.mult)
                    V.tensor_tensor(per_head(k_beta), per_head(bank[4]), over_cols(beta_dec[:, four]), ALU.mult)
                    for c, (qd, kd) in enumerate(((q_first, k_first), (q_second, k_second))):
                        of = slice(c * CHUNK, (c + 1) * CHUNK)
                        V.tensor_tensor(per_head(kd)[of], per_head(bank[4])[of], over_cols(dec_end[of, four]), ALU.mult)
                        m = V.tensor_tensor(per_head(qd)[:, :, of], q_all[:, :, ds(t * P + c * CHUNK, CHUNK)], per_head(row_dec)[:, :, of], ALU.mult)
                    m.then_inc(S["tokens_made"], 1)
                    dve.wait_ge(S["inv_made"], t + 1)
                    for n in range(NL):
                        dve.wait_ge(S["corr_made"], t * NL + n + 1)
                        if n < NL - 1:
                            V.tensor_tensor(inv, inv, bank[7], ALU.subtract)
                        V.tensor_tensor(inv_t, inv_t, bank[6], ALU.subtract).then_inc(S["level_done"], 1)
                        dve.wait_ge(S["level_done"], t * NL + n + 1)
                    dve.wait_ge(S["uw_kept"], t + 1)
                    for c, (old, new) in enumerate(((state, middle), (middle, state))):
                        of = slice(c * CHUNK, (c + 1) * CHUNK)
                        dve.wait_ge(S["ws_made"], t * 2 + c + 1)
                        V.tensor_tensor(v_new[of], u_tile[of], bank[4][of], ALU.subtract).then_inc(S["v_new_made"], 1)
                        dve.wait_ge(S["gain_made"], t * 2 + c + 1)
                        if c == 1:
                            dve.wait_ge(S["o_made"], t + 1)
                        end = (c + 1) * CHUNK - 1
                        for h in range(HEADS):
                            cols = slice(h * P, (h + 1) * P)
                            m = V.scalar_tensor_tensor(new[:, cols], old[:, cols], row_dec[:, h * P + end:h * P + end + 1],
                                                       bank[5][:, cols], ALU.mult, ALU.add)
                        m.then_inc(S["state_made"], 1)
                        dve.wait_ge(S["state_made"], t * 2 + c + 1)

            @block.tensor
            def _(pe):
                def heads(to, left, right):
                    for h in range(HEADS):
                        c = slice(h * P, (h + 1) * P)
                        m = PE.matmul(to[:, c], left[:, c], right[:, c], start=True, stop=True)
                    return m

                def turn(to, of):
                    for h in range(HEADS):
                        c = slice(h * P, (h + 1) * P)
                        m = PE.transpose(to[:, c], of[:, c], ident)
                    return m

                pe.wait_ge(S["zeroed"], 1)
                with pe.Fori(0, TILES) as t:
                    pe.wait_ge(S["sum_rhs_made"], t + 1)
                    pe.wait_ge(S["beta_rhs_made"], t + 1)
                    pe.wait_ge(S["state_made"], t * 2)
                    pe.wait_ge(S["o_kept"], t)
                    PE.matmul(bank[0], ones, sum_rhs, start=True, stop=True)
                    PE.matmul(bank[1], ones, beta_rhs, start=True, stop=True).then_inc(S["rows_made"], 1)
                    pe.wait_ge(S["kv_kept"], t + 1)
                    heads(bank[2], k_tile, k_tile)
                    for h in range(HEADS):
                        c = slice(h * P, (h + 1) * P)
                        m = PE.matmul(bank[3][:, c], k_tile[:, c], q_all[:, h, ds(t * P, P)], start=True, stop=True)
                    m.then_inc(S["kk_made"], 1)
                    turn(bank[4], k_tile)
                    turn(bank[5], v_tile).then_inc(S["turned_kv"], 1)
                    pe.wait_ge(S["inv_t_made"], t + 1)
                    turn(bank[6], inv_t).then_inc(S["inv_turned"], 1)
                    pe.wait_ge(S["inv_made"], t + 1)
                    for n in range(NL):
                        pe.wait_ge(S["lower_made"], t * NL + n + 1)
                        pe.wait_ge(S["level_done"], t * NL + n)
                        heads(bank[6], lower[n], inv).then_inc(S["prod_made"], 1)
                        pe.wait_ge(S["prod_kept"], t * NL + n + 1)
                        if n < NL - 1:
                            heads(bank[7], inv_t, prod)
                        heads(bank[6], prod, inv_t).then_inc(S["corr_made"], 1)
                    pe.wait_ge(S["level_done"], t * NL + NL)
                    pe.wait_ge(S["tokens_made"], t + 1)
                    heads(bank[2], inv_t, v_beta)
                    heads(bank[3], k_beta, inv_t).then_inc(S["uw_made"], 1)
                    pe.wait_ge(S["uw_kept"], t + 1)
                    for c, (old, k_chunk) in enumerate(((state, k_first), (middle, k_second))):
                        if c == 1:
                            pe.wait_ge(S["state_made"], t * 2 + 1)
                        heads(bank[4], w_tile, old).then_inc(S["ws_made"], 1)
                        pe.wait_ge(S["v_new_made"], t * 2 + c + 1)
                        heads(bank[5], k_chunk, v_new).then_inc(S["gain_made"], 1)
                    for h in range(HEADS):
                        c = slice(h * P, (h + 1) * P)
                        PE.matmul(bank[7][:, c], q_first[:, c], state[:, c], start=True, stop=False)
                        PE.matmul(bank[7][:, c], q_second[:, c], middle[:, c], start=False, stop=False)
                        m = PE.matmul(bank[7][:, c], scores[:, c], v_new[:, c], start=False, stop=True)
                    m.then_inc(S["o_made"], 1)

        w_out = hn_t
        cut = Cut(work[:, mix.at:])
        o_spare = Cut(work[:, 0:N_MASKS])
        gated, mixed_g = o_spare(HALF), o_spare(HALF)
        squares, mixed_p = cut(HALF), cut(HALF)
        o_stat = cut(3 * TH)
        w_query = [cut(DM + NKEYS) for _ in range(2)]
        w_out_in, w_query_in = sem("w_out_in"), [sem(f"w_query_in{n}") for n in range(2)]
        names = ("key_product", "w_score_kept", "h_squares", "h_means", "h_roots", "squares", "squares_used", "means", "roots", "rstds", "z_silu", "gated", "turned", "turned_kept", "pool_kept", "projected", "summed")
        M = {n: sem("m_" + n) for n in names}
        with nc.Block() as block:
            @block.sync
            def _(sp):
                sp.dma_start(w_out, a["w_out"]).then_inc(w_out_in, 16)
                for s in range(2):
                    sp.dma_start(w_query[s], a["w_query"][s, :, :]).then_inc(w_query_in[s], 16)
                with sp.Fori(0, PHEADS - 1) as i:
                    for s in range(2):
                        sp.wait_ge(M["key_product"], i * 2 + (s + 1))
                        sp.dma_start(w_query[s], a["w_query"][ds(i * 2 + (s + 2), 1), :, :].rearrange("a p c -> p (a c)")).then_inc(w_query_in[s], 16)

            @block.scalar
            def _(act):
                with act.Fori(0, TILES) as t:
                    act.wait_ge(M["squares_used"], t)
                    A.activation(squares, o_all[:, ds(t * HALF, HALF)], ACT.Square).then_inc(M["squares"], 1)
                act.wait_ge(M["means"], 1)
                A.activation(o_stat[:, TH:2 * TH], o_stat[:, 0:TH], ACT.Sqrt).then_inc(M["roots"], 1)
                with act.Fori(0, TILES) as t:
                    at = z_all[:, ds(t * HALF, HALF)]
                    A.activation(at, at, ACT.Silu).then_inc(M["z_silu"], 1)
                    act.wait_ge(M["turned"], t + 1)
                    act.wait_ge(M["projected"], t)
                    A.activation(mixed_g, bank[2], ACT.Copy).then_inc(M["turned_kept"], 1)
                    for s in range(2):
                        act.wait_ge(M["key_product"], t * 2 + (s + 1))
                        to = w_score.rearrange("p (d k) -> p d k", d=DB)[:, :, ds(t * QD + s * P, P)]
                        A.activation(to[:, 0:4, :], bank[4 + 2 * s].rearrange("p (d k) -> p d k", d=4), ACT.Copy)
                        A.activation(to[:, 4:8, :], bank[5 + 2 * s].rearrange("p (d k) -> p d k", d=4), ACT.Copy).then_inc(M["w_score_kept"], 1)
                    act.wait_ge(M["summed"], t + 1)
                    for half, used in enumerate((o_all, z_all)):
                        m = A.activation(used[:, ds(t * HALF, HALF)], h_all[:, ds(t * DM + half * HALF, HALF)], ACT.Square,
                                         accum_out=stat[:, ds(t + half * 8, 1)])
                    m.then_inc(M["h_squares"], 1)
                    act.wait_ge(M["h_squares"], t + 1)
                act.wait_ge(M["h_means"], 1)
                A.activation(stat[:, 16:24], stat[:, 8:16], ACT.Sqrt).then_inc(M["h_roots"], 1)

            @block.vector
            def _(dve):
                with vc.loop(0, TILES, 0) as t:
                    dve.wait_ge(M["squares"], t + 1)
                    V.tensor_reduce(o_stat[:, ds(t * HEADS, HEADS)], per_head(squares), AX.X, ALU.add).then_inc(M["squares_used"], 1)
                dve.wait_ge(M["squares_used"], TILES)
                V.tensor_scalar(o_stat[:, 0:TH], o_stat[:, 0:TH], 1.0 / HD, EPS, ALU.mult, ALU.add).then_inc(M["means"], 1)
                dve.wait_ge(M["roots"], 1)
                V.reciprocal(o_stat[:, 2 * TH:3 * TH], o_stat[:, TH:2 * TH]).then_inc(M["rstds"], 1)
                dve.wait_ge(M["rstds"], 1)
                with vc.loop(0, TILES, 2) as t:
                    dve.wait_ge(M["turned"], t)
                    vc.link(V.tensor_tensor(per_head(gated), per_head(o_all[:, ds(t * HALF, HALF)]), over_cols(o_stat[:, ds(t * HEADS + 2 * TH, HEADS)]), ALU.mult))
                    vc.link(V.tensor_tensor(per_head(gated), per_head(gated), over_heads(out_gain), ALU.mult))
                    dve.wait_ge(M["z_silu"], t + 1)
                    V.tensor_tensor(gated, gated, z_all[:, ds(t * HALF, HALF)], ALU.mult).then_inc(M["gated"], 1)
                    dve.wait_ge(M["projected"], t + 1)
                    for half in range(2):
                        at = h_all[:, ds(t * DM + half * HALF, HALF)]
                        m = V.tensor_tensor(at, bank[half], at, ALU.add)
                    m.then_inc(M["summed"], 1)
                    dve.wait_ge(M["summed"], t + 1)
                dve.wait_ge(M["h_squares"], TILES)
                vc.link(V.tensor_tensor(stat[:, 0:8], stat[:, 0:8], stat[:, 8:16], ALU.add))
                V.tensor_scalar(stat[:, 8:16], stat[:, 0:8], 1.0 / DM, EPS, ALU.mult, ALU.add).then_inc(M["h_means"], 1)
                dve.wait_ge(M["h_roots"], 1)
                vc.link(V.reciprocal(ffn_rstd, stat[:, 16:24]))

            @block.tensor
            def _(pe):
                pe.wait_ge(w_out_in, 16)
                with pe.Fori(0, TILES) as t:
                    pe.wait_ge(M["gated"], t + 1)
                    pe.wait_ge(M["turned_kept"], t)
                    for h in range(HEADS):
                        c = slice(h * P, (h + 1) * P)
                        m = PE.transpose(bank[2][:, c], gated[:, c], ident)
                    m.then_inc(M["turned"], 1)
                    pe.wait_ge(M["turned_kept"], t + 1)
                    pe.wait_ge(M["pool_kept"], t + 1)
                    pe.wait_ge(M["summed"], t)
                    for half in range(2):
                        for d in range(DB):
                            src = mixed_p if d < 4 else mixed_g
                            m = PE.matmul(bank[half], src[:, (d % 4) * P:(d % 4 + 1) * P],
                                          w_out[:, d * DM + half * HALF:d * DM + (half + 1) * HALF], start=(d == 0), stop=(d == DB - 1))
                    m.then_inc(M["projected"], 1)
                    for s in range(2):
                        pe.wait_ge(w_query_in[s], t * 16 + 16)
                        pe.wait_ge(M["w_score_kept"], t * 2)
                        for d in range(DB):
                            m = PE.matmul(bank[4 + 2 * s + d // 4][:, (d % 4) * P:(d % 4 + 1) * P], w_query[s][:, d * P:(d + 1) * P],
                                          w_query[s][:, DM:], start=True, stop=True)
                        m.then_inc(M["key_product"], 1)

            @block.gpsimd
            def _(pool):
                with pool.Fori(0, TILES) as t:
                    pool.wait_ge(M["projected"], t)
                    pool.sem_inc(pool_steps, 1)
                    G.tensor_copy(per_head(mixed_p), pool_t.rearrange("p (g s) -> p g s", g=4)[:, :, ds(t * P, P)]).then_inc(M["pool_kept"], 1)

        cut = Cut(work)
        hf_now, hf_next, hf_t, out_tile = cut(DM), cut(DM), cut(DM), cut(DM)
        diag = [cut(P) for _ in range(RING)]
        picks = cut(TILES * PICKS).bitcast(I32)
        pick_now = cut(TOPK).bitcast(I32)
        gates, gate_sum, gate_scale = cut(PICKS), cut(PHEADS), cut(PHEADS)
        val, ix, ix_f = cut(2 * TOPK), cut(2 * TOPK).bitcast(U32), cut(2 * TOPK)
        left, pairs = cut(2 * P), cut(2 * P)
        pos, pos_hl, pos_f = cut(TOPK).bitcast(U32), cut(2 * TOPK).bitcast(U32), cut(2 * TOPK)
        same, found = cut(2 * TOPK * TOPK), cut(2 * TOPK)
        dots, scored_gelu, weights = cut(TOPK), cut(TOPK), cut(TOPK)
        f_stat = stat[:, 0:4]
        ring = [ring_mem[:, n * 2 * DM:(n + 1) * 2 * DM] for n in range(RING)]
        names = ("hf_made", "hf_turned", "hf_kept", "scored", "picked", "gates_made", "used", "dot_made", "gelu_made",
                 "weights_made", "diag_made", "summed", "f_sumsq", "f_mean", "f_root", "out_made", "out_stored", "picks_now")
        X = {n: sem("x_" + n) for n in names}
        got = [sem(f"got{n}") for n in range(RING)]
        vector_steps, tensor_steps = sem("vector_steps"), sem("tensor_steps")
        USED0 = TOPK
        GROUPS = TOPK // GROUP
        AHEAD = 2
        TURN = PHEADS - AHEAD - 1
        START, END = 0, PHEADS - 1

        def at(j, head):
            return isinstance(j, int) and j == head

        with nc.Block() as block:
            @block.gpsimd
            def _(pool):
                with pool.Fori(0, TILES) as t:
                    pool.sem_inc(pool_steps, 1)
                    with pool.Fori(0, PHEADS) as j:
                        pool.wait_ge(X["picked"], t * PHEADS + (j + 1))
                        pool.sem_inc(pool_steps, 1)
                        for half in range(2):
                            pool.wait_ge(X["used"], t * PICKS + j * TOPK + (USED0 - TOPK + 8 * half + 8))
                            pool.sem_inc(pool_steps, 1)
                            G.tensor_copy(pick_now[:, half * 8:half * 8 + 8],
                                          picks[:, ds(t * PICKS + j * TOPK + half * 8, 8)]).then_inc(X["picks_now"], 1)
                            pool.wait_ge(X["picks_now"], t * (2 * PHEADS) + j * 2 + (half + 1))
                            pool.sem_inc(pool_steps, 1)
                            for k in range(half * 8, half * 8 + 8):
                                pool.wait_ge(X["used"], t * PICKS + j * TOPK + (USED0 + k - RING + 1))
                                pool.sem_inc(pool_steps, 1)
                                G.indirect_dma_start(ring[k % RING], None, a["experts"],
                                                     bass.IndirectOffsetOnAxis(ap=pick_now[:, k:k + 1], axis=0)).then_inc(got[k % RING], 16)

            @block.sync
            def _(sp):
                with sp.Fori(0, TILES) as t:
                    sp.wait_ge(X["out_made"], t + 1)
                    sp.dma_start(out[ds(t * P, P), :], out_tile).then_inc(X["out_stored"], 16)
                sp.wait_ge(X["out_stored"], 16 * TILES)

            @block.scalar
            def _(act):
                def turned(t):
                    act.wait_ge(X["hf_turned"], t + 1)
                    A.activation(hf_t[:, 0:HALF], bank[0], ACT.Copy)
                    A.activation(hf_t[:, HALF:DM], bank[1], ACT.Copy).then_inc(X["hf_kept"], 1)

                def gate(n, j):
                    act.wait_ge(X["picked"], n + 1)
                    part = gates[:, ds(j * TOPK, TOPK)]
                    A.activation(part, part, ACT.Exp, accum_out=gate_sum[:, ds(j, 1)]).then_inc(X["gates_made"], 1)

                def final_sum(t):
                    act.wait_ge(X["summed"], t + 1)
                    act.wait_ge(X["out_stored"], t * 16)
                    A.activation(out_tile, h_all[:, ds(t * DM, DM)], ACT.Square, accum_out=f_stat[:, 0:1]).then_inc(X["f_sumsq"], 1)

                def final_root(t):
                    act.wait_ge(X["f_mean"], t + 1)
                    A.activation(f_stat[:, 2:3], f_stat[:, 1:2], ACT.Sqrt).then_inc(X["f_root"], 1)

                def step(t, j, first, last, jn):
                    for m in range(GROUPS):
                        of = slice(m * GROUP, (m + 1) * GROUP)
                        act.wait_ge(X["dot_made"], t * PICKS + j * TOPK + (m + 1) * GROUP)
                        A.activation(scored_gelu[:, of], dots[:, of], ACT.Gelu).then_inc(X["gelu_made"], 1)
                        act.wait_ge(X["weights_made"], t * (PHEADS * GROUPS) + j * GROUPS + (m + 1))
                        for k in range(m * GROUP, (m + 1) * GROUP):
                            act.wait_ge(X["used"], t * PICKS + j * TOPK + (USED0 + k - RING + 1))
                            A.activation(diag[k % RING], ident, ACT.Copy, scale=weights[:, k:k + 1]).then_inc(X["diag_made"], 1)
                        if m == 1 and jn is not None:
                            gate(t * PHEADS + (j + 1), jn)
                        if m == 1 and at(j, TURN) and not last:
                            turned(t + 1)
                        if at(j, START) and not first:
                            if m == 0:
                                final_sum(t - 1)
                            if m == 1:
                                final_root(t - 1)

                def tile(t, first=False, last=False):
                    step(t, START, first, last, 1)
                    with act.Fori(1, TURN) as j:
                        step(t, j, first, last, j + 1)
                    for j in range(TURN, PHEADS - 1):
                        step(t, j, first, last, j + 1)
                    step(t, PHEADS - 1, first, last, None if last else 0)

                turned(0)
                gate(0, 0)
                tile(0, first=True)
                with act.Fori(1, TILES - 1) as t:
                    tile(t)
                tile(TILES - 1, last=True)
                final_sum(TILES - 1)
                final_root(TILES - 1)

            @block.vector
            def _(dve):
                def link_held(instruction):
                    vc.link(instruction)
                    V.sem_inc(vector_steps, 1)

                def query(t):
                    V.scalar_tensor_tensor(hf_next, h_all[:, ds(t * DM, DM)], ffn_rstd[:, ds(t, 1)], gain_ffn,
                                           ALU.mult, ALU.mult).then_inc(X["hf_made"], 1)

                def top16(values, indices, src, rest):
                    link_held(V.max(values[:, 0:8], src))
                    V.max_index(indices[:, 0:8], values[:, 0:8], src)
                    link_held(V.match_replace(rest, values[:, 0:8], src, LOW))
                    link_held(V.max(values[:, 8:16], rest))
                    link_held(V.max_index(indices[:, 8:16], values[:, 8:16], rest))

                def pick(piece, t, j, jp):
                    n = t * PHEADS + (j + AHEAD)
                    if piece < 2:
                        of = slice(piece * TOPK, (piece + 1) * TOPK)
                        if piece == 0:
                            dve.wait_ge(X["scored"], n + 1)
                            V.sem_inc(vector_steps, 1)
                        top16(val[:, of], ix[:, of], bank[2][:, piece * P:(piece + 1) * P], left[:, 0:P])
                    elif piece == 2:
                        link_held(V.tensor_tensor(pairs.rearrange("p (i k) -> p i k", i=TOPK),
                                                  val[:, 0:TOPK].unsqueeze(2).to_broadcast([P, TOPK, TOPK]),
                                                  val[:, TOPK:].unsqueeze(1).to_broadcast([P, TOPK, TOPK]), ALU.add))
                        top16(val[:, 0:TOPK], pos, pairs, left)
                    else:
                        V.tensor_scalar(gates[:, ds(jp * TOPK, TOPK)], val[:, 0:TOPK], val[:, 0:1], None, ALU.subtract)
                        V.tensor_copy(ix_f, ix)
                        V.tensor_scalar(pos_hl[:, 0:TOPK], pos, 4, None, ALU.logical_shift_right)
                        vc.link(V.tensor_scalar(pos_hl[:, TOPK:], pos, TOPK - 1, None, ALU.bitwise_and))
                        vc.link(V.tensor_copy(pos_f, pos_hl))
                        three = same.rearrange("p (k i) -> p k i", i=TOPK)
                        vc.link(V.tensor_tensor(three, pos_f.unsqueeze(2).to_broadcast([P, 2 * TOPK, TOPK]),
                                                iota.unsqueeze(1).to_broadcast([P, 2 * TOPK, TOPK]), ALU.is_equal))
                        for h in range(2):
                            part = three[:, h * TOPK:(h + 1) * TOPK, :]
                            m = V.tensor_tensor(part, part, ix_f[:, h * TOPK:(h + 1) * TOPK].unsqueeze(1).to_broadcast([P, TOPK, TOPK]), ALU.mult)
                        vc.link(m)
                        vc.link(V.tensor_reduce(found, three, AX.X, ALU.add))
                        V.scalar_tensor_tensor(picks[:, ds(t * PICKS + (j * TOPK + AHEAD * TOPK), TOPK)], found[:, 0:TOPK], float(NKEYS),
                                               found[:, TOPK:], ALU.mult, ALU.add).then_inc(X["picked"], 1)
                        dve.wait_ge(X["picked"], n + 1)

                def gate(n, j):
                    dve.wait_ge(X["gates_made"], n + 1)
                    vc.link(V.reciprocal(gate_scale[:, ds(j, 1)], gate_sum[:, ds(j, 1)]))

                def take_sum(t):
                    dve.wait_ge(X["used"], t * PICKS + (USED0 + PICKS))
                    for half in range(2):
                        h = h_all[:, ds(t * DM + half * HALF, HALF)]
                        m = V.tensor_tensor(h, bank[6 + half], h, ALU.add)
                    m.then_inc(X["summed"], 1)

                def final_mean(t):
                    dve.wait_ge(X["f_sumsq"], t + 1)
                    V.tensor_scalar(f_stat[:, 1:2], f_stat[:, 0:1], 1.0 / DM, EPS, ALU.mult, ALU.add).then_inc(X["f_mean"], 1)

                def final_out(t):
                    dve.wait_ge(X["f_root"], t + 1)
                    vc.link(V.reciprocal(f_stat[:, 3:4], f_stat[:, 2:3]))
                    V.scalar_tensor_tensor(out_tile, h_all[:, ds(t * DM, DM)], f_stat[:, 3:4], gain_fin, ALU.mult, ALU.mult).then_inc(X["out_made"], 1)

                def step(t, j, first, last, jp, jn):
                    if at(j, START):
                        if not first:
                            dve.wait_ge(X["dot_made"], t * PICKS)
                        vc.link(V.scalar_tensor_tensor(hf_now, h_all[:, ds(t * DM, DM)], ffn_rstd[:, ds(t, 1)], gain_ffn, ALU.mult, ALU.mult))
                    for m in range(GROUPS):
                        for k in range(m * GROUP, (m + 1) * GROUP):
                            dve.wait_ge(got[k % RING], t * (PICKS * 16 // RING) + j * (TOPK * 16 // RING) + 16 * (k // RING + 1))
                            row = ring[k % RING][:, 0:DM]
                            V.tensor_tensor_reduce(out=row, in0=row, in1=hf_now, scale=1.0, scalar=0.0, op0=ALU.mult, op1=ALU.add,
                                                   accum_out=dots[:, k:k + 1]).then_inc(X["dot_made"], 1)
                        of = slice(m * GROUP, (m + 1) * GROUP)
                        made = t * (PHEADS * GROUPS) + j * GROUPS + (m + 1)
                        dve.wait_ge(X["gelu_made"], made)
                        V.scalar_tensor_tensor(weights[:, of], scored_gelu[:, of], gate_scale[:, ds(j, 1)],
                                               gates[:, ds(j * TOPK + m * GROUP, GROUP)], ALU.mult, ALU.mult).then_inc(X["weights_made"], 1)
                        if at(j, START) and not first:
                            if m == 0:
                                take_sum(t - 1)
                            if m == 1:
                                final_mean(t - 1)
                            if m == 2:
                                final_out(t - 1)
                        if jp is not None:
                            pick(m, t, j, jp)
                        if m == 2 and jn is not None:
                            gate(t * PHEADS + (j + 1), jn)
                        if m == 3 and at(j, START) and not last:
                            dve.wait_ge(X["hf_turned"], t + 1)
                            query(t + 1)

                def tile(t, first=False, last=False):
                    step(t, START, first, last, AHEAD, 1)
                    V.sem_inc(vector_steps, 1)
                    with vc.loop(1, TURN, PICK_LINKS + 1) as j:
                        step(t, j, first, last, j + AHEAD, j + 1)
                    for j in range(TURN, PHEADS):
                        jp = None if last and j > TURN else (j + AHEAD) % PHEADS
                        jn = None if last and j == PHEADS - 1 else (j + 1) % PHEADS
                        step(t, j, first, last, jp, jn)

                PICK_LINKS = 18
                dve.wait_ge(gains_in, 32)
                V.memset(dots, 0.0).then_inc(X["used"], USED0)
                query(0)
                for n in range(AHEAD):
                    for piece in range(4):
                        pick(piece, 0, n - AHEAD, n)
                gate(0, 0)
                tile(0, first=True)
                with vc.loop(1, TILES - 1, PHEADS * (PICK_LINKS + 1) + 2) as t:
                    tile(t)
                tile(TILES - 1, last=True)
                take_sum(TILES - 1)
                final_mean(TILES - 1)
                final_out(TILES - 1)

            @block.tensor
            def _(pe):
                def turn(t):
                    pe.wait_ge(X["hf_made"], t + 1)
                    for d in range(DB):
                        m = PE.transpose(bank[d // 4][:, (d % 4) * P:(d % 4 + 1) * P], hf_next[:, d * P:(d + 1) * P], ident)
                    m.then_inc(X["hf_turned"], 1)

                def head(n, j):
                    pe.wait_ge(X["picked"], n)
                    for d in range(DB):
                        m = PE.matmul(bank[2][:, 0:QD], hf_t[:, d * P:(d + 1) * P],
                                      w_score[:, ds(j * QD + d * (PHEADS * QD), QD)], start=(d == 0), stop=(d == DB - 1))
                    m.then_inc(X["scored"], 1)

                def step(t, j, first, last, jp):
                    if jp is not None:
                        head(t * PHEADS + (j + AHEAD), jp)
                    if at(j, START) and not first:
                        pe.wait_ge(X["summed"], t + 0)
                    for k in range(TOPK):
                        pe.wait_ge(X["diag_made"], t * PICKS + j * TOPK + (k + 1))
                        for half in range(2):
                            m = PE.matmul(bank[6 + half], diag[k % RING], ring[k % RING][:, DM + half * HALF:DM + (half + 1) * HALF],
                                          start=(at(j, START) and k == 0), stop=(at(j, END) and k == TOPK - 1))
                        m.then_inc(X["used"], 1)
                        if k == GROUP - 1 and at(j, TURN) and not last:
                            turn(t + 1)

                def tile(t, first=False, last=False):
                    step(t, START, first, last, AHEAD)
                    with pe.Fori(1, TURN) as j:
                        step(t, j, first, last, j + AHEAD)
                    step(t, TURN, first, last, TURN + AHEAD)
                    if not last:
                        pe.wait_ge(X["hf_kept"], t + 2)
                        pe.sem_inc(tensor_steps, 1)
                    for j in range(TURN + 1, PHEADS):
                        step(t, j, first, last, None if last else j + AHEAD - PHEADS)

                turn(0)
                pe.wait_ge(X["hf_kept"], 1)
                pe.sem_inc(tensor_steps, 1)
                for n in range(AHEAD):
                    head(n, n)
                tile(0, first=True)
                with pe.Fori(1, TILES - 1) as t:
                    tile(t)
                tile(TILES - 1, last=True)
    return nc


def kernel(x, norm_mix_gain, w_in, conv_w, a_log, dt_bias, gdn_out_gain, w_pool, b_pool, pool_scale, w_out,
           norm_ffn_gain, peer_w_query, peer_sub_keys_1, peer_sub_keys_2, peer_expert_u, peer_expert_v,
           norm_final_gain):
    import concourse.bacc as bacc
    from concourse.bass_utils import run_bass_kernel_spmd

    data = layout(x, norm_mix_gain, w_in, conv_w, a_log, dt_bias, gdn_out_gain, w_pool, b_pool, pool_scale, w_out,
                  norm_ffn_gain, peer_w_query, peer_sub_keys_1, peer_sub_keys_2, peer_expert_u, peer_expert_v,
                  norm_final_gain)
    nc = bacc.Bacc("TRN2", target_bir_lowering=False, num_devices=1)
    ins = {n: nc.dram_tensor("in_" + n, v.shape, mybir.dt.from_np(v.dtype), kind="ExternalInput").ap() for n, v in data.items()}
    out = nc.dram_tensor("out", (SEQ, DM), mybir.dt.float32, kind="ExternalOutput").ap()
    build(nc, ins, out)
    r = run_bass_kernel_spmd(nc, [{"in_" + n: v for n, v in data.items()}], core_ids=[0])
    return r.results[0]["out"].reshape(1, SEQ, DM)


def layout(x, norm_mix_gain, w_in, conv_w, a_log, dt_bias, gdn_out_gain, w_pool, b_pool, pool_scale, w_out,
           norm_ffn_gain, peer_w_query, peer_sub_keys_1, peer_sub_keys_2, peer_expert_u, peer_expert_v,
           norm_final_gain):
    def rows(w):
        w = np.asarray(w)
        return w.reshape(-1, P, w.shape[1]).transpose(1, 0, 2).reshape(P, -1)

    w_in = np.asarray(w_in)[0]
    n_mixed = HALF + 3 * HALF
    wc = w_in[:, :n_mixed].reshape(DB, P, n_mixed // P, P).transpose(2, 1, 0, 3).reshape(n_mixed // P, P, DM)
    taps = np.asarray(conv_w)[0].reshape(TAPS, 12, P).transpose(2, 1, 0).reshape(P, 12 * TAPS)
    keys = np.stack([np.asarray(peer_sub_keys_1)[0], np.asarray(peer_sub_keys_2)[0]], axis=1)
    data = {
        "x": np.asarray(x)[0],
        "constants": constants(),
        "gain_mix": np.asarray(norm_mix_gain)[0],
        "gain_ffn": np.asarray(norm_ffn_gain)[0],
        "gain_fin": np.asarray(norm_final_gain),
        "out_gain": np.asarray(gdn_out_gain)[0],
        "wc": wc,
        "wz": rows(w_in[:, n_mixed:n_mixed + HALF]),
        "wab": rows(w_in[:, n_mixed + HALF:]),
        "per_channel": np.concatenate([taps, np.asarray(b_pool)[0].T, np.asarray(pool_scale)[0].reshape(4, P).T], axis=1),
        "per_head": np.concatenate([np.asarray(a_log)[0], np.asarray(dt_bias)[0]]),
        "w_pool": np.asarray(w_pool)[0].transpose(1, 0, 2).reshape(P, 4 * P),
        "w_out": rows(np.asarray(w_out)[0]),
        "w_query": np.concatenate([np.asarray(peer_w_query)[0].reshape(DM, 2 * PHEADS, P).transpose(1, 2, 0),
                                   keys.reshape(2 * PHEADS, NKEYS, P).transpose(0, 2, 1)], axis=2),
        "experts": np.concatenate([np.asarray(peer_expert_u)[0], np.asarray(peer_expert_v)[0]], axis=1),
    }
    return {n: np.ascontiguousarray(v) for n, v in data.items()}
```

```python
from contextlib import ExitStack, contextmanager

import numpy as np

import concourse.bass as bass
from concourse import mybir

P = 128
SEQ, DM = 1024, 1024
TILES = SEQ // P
DB = DM // P
CHUNK = 64
HALF = 512
HEADS = 4
HD = 128
POOL_WINDOWS = (2, 4, 8, 16)
PAD = 16
TAPS = 4
EPS = 1e-6
PHEADS, NKEYS, TOPK = 8, 128, 16
QD = 2 * P
PICKS = PHEADS * TOPK
LEVELS = (2, 4, 8, 16, 32)
RING = 8
GROUP = 4
LOW = -3.0e38


class Chain:

    def __init__(self, engine, sem):
        self.engine, self.sem, self.base, self.n = engine, sem, 0, 0

    def link(self, instruction):
        self.n += 1
        instruction.then_inc(self.sem, 1)
        self.engine.wait_ge(self.sem, self.base + self.n)

    @contextmanager
    def loop(self, first, end, links):
        base, n = self.base, self.n
        with self.engine.Fori(first, end) as i:
            if links:
                self.base, self.n = i * links + (base + n - first * links), 0
            yield i
            assert self.n - (0 if links else n) == links, f"the body makes {self.n} links"
        self.base, self.n = base, n + (end - first) * links


class Cut:

    def __init__(self, ap):
        self.ap, self.at = ap, 0

    def __call__(self, cols):
        self.at += cols
        assert self.at <= self.ap.shape[1], (self.at, self.ap.shape)
        return self.ap[:, self.at - cols:self.at]


def constants():
    j, i = np.arange(P)[:, None], np.arange(P)[None, :]
    same = (j // CHUNK) == (i // CHUNK)
    cols = [j == i, np.broadcast_to(np.arange(TOPK), (P, TOPK)),
            np.ones((P, P)), same & (j <= i), same & (j > i)]
    for s in (1,) + LEVELS:
        cols.append((j // (2 * s) == i // (2 * s)) & (j % (2 * s) < s) & (i % (2 * s) >= s))
    for w in POOL_WINDOWS:
        cols.append(np.broadcast_to(1.0 / np.minimum(np.arange(PAD) + 1, w), (P, PAD)))
    return np.concatenate([c.astype(np.float32) for c in cols], axis=1)


N_KEPT = P + TOPK
N_MASKS = (3 + 1 + len(LEVELS)) * P + len(POOL_WINDOWS) * PAD


def build(nc, a, out):
    F32, I32, U32 = mybir.dt.float32, mybir.dt.int32, mybir.dt.uint32
    ALU, ACT, AX = mybir.AluOpType, mybir.ActivationFunctionType, mybir.AxisListType
    PE, V, A, G = nc.tensor, nc.vector, nc.scalar, nc.gpsimd
    ds = bass.ds
    top = ExitStack()

    def sb(name, cols, dtype=F32):
        return top.enter_context(nc.sbuf_tensor(name, [P, cols], dtype))[:, :]

    def sem(name):
        return top.enter_context(nc.semaphore(name))

    def per_head(ap):
        return ap.rearrange("p (h c) -> p h c", h=HEADS)

    def over_heads(ap):
        return ap.unsqueeze(1).to_broadcast([P, HEADS, P])

    def over_cols(ap, cols=P):
        return ap.unsqueeze(2).to_broadcast([ap.shape[0], ap.shape[1], cols])

    with top:
        bank = [top.enter_context(nc.psum_tensor(f"bank{n}", [P, HALF], F32))[:, :] for n in range(8)]
        pool_steps, vector_steps, tensor_steps, scalar_steps = (sem(n + "_steps") for n in ("pool", "vector", "tensor", "scalar"))
        vc = Chain(V, sem("vector_chain"))

        kept = sb("kept", N_KEPT)
        ident, iota = kept[:, 0:P], kept[:, P:P + TOPK]
        x_all = sb("x_all", TILES * DM)
        gain_ffn = sb("gain_ffn", DM)
        gain_fin = sb("gain_fin", DM)
        stat = sb("stat", 32)
        eps_col = sb("eps_col", 1)
        late = sb("late", 2 * 8 * DM)
        ring_mem = sb("ring_mem", RING * 2 * DM)
        work = sb("work", 9900)

        w_out = x_all
        w_score = late
        qkv_t = late[:, 0:12 * SEQ]
        z_all = ring_mem[:, 0:TILES * HALF]
        o_all = ring_mem[:, TILES * HALF:2 * TILES * HALF]
        hn_t = ring_mem[:, 2 * TILES * HALF:2 * TILES * HALF + DB * SEQ]

        mix = Cut(work)
        masks = mix(N_MASKS)
        ones, causal, after = (masks[:, n * P:(n + 1) * P] for n in range(3))
        level_mask = [masks[:, (3 + n) * P:(4 + n) * P] for n in range(6)]
        inv_count = masks[:, 9 * P:]
        small = mix(64)
        conv_w, b_pool, pool_scale = small[:, 0:48], small[:, 48:52], small[:, 52:56]
        a_log, dt_bias = small[:, 56:60], small[:, 60:64]
        out_gain = mix(HD)
        ab_all = mix(TILES * 8)
        o_stat = mix(3 * TILES * HEADS)
        pool_t = mix(4 * SEQ)

        early = Cut(late[:, 0:12 * SEQ])
        wz, wab, gain_mix, hn, junk = early(DB * HALF), early(DB * 8), early(DM), early(DM), early(DM)
        hn_tile = [early(DM) for _ in range(2)]
        wc = [late[:, 12 * SEQ + n * DM:12 * SEQ + (n + 1) * DM] for n in range(4)]
        wc_in = [sem(f"wc_in{n}") for n in range(4)]
        x_first_in, x_in, const_in, wz_in, small_in, gains_in = (
            sem(n) for n in ("x_first_in", "x_in", "const_in", "wz_in", "small_in", "gains_in"))
        sq_made, ms_made, root_made, rstd_made = (sem(n) for n in ("sumsq_made", "mean_made", "root_made", "rstd_made"))
        hn_made, turned, tile_kept, z_made, z_kept, hn_kept = (
            sem(n) for n in ("hn_made", "hn_turned", "hn_tile_kept", "z_made", "z_kept", "hn_kept"))

        def norm_steps(loop, step):
            with loop(0, TILES // 2 - 1) as i:
                for s in range(2):
                    step(i * 2 + s, s, 2)
            step(TILES - 2, 0, 1)
            step(TILES - 1, 1, 0)

        with nc.Block() as block:
            @block.sync
            def _(sp):
                sp.dma_start(x_all[:, 0:2 * DM].rearrange("p (t d) -> p t d", t=2),
                             a["x"][0:2 * P, :].rearrange("(t p) d -> p t d", p=P)).then_inc(x_first_in, 16)
                sp.dma_start(gain_mix, a["gain_mix"].partition_broadcast(P)).then_inc(const_in, 16)
                sp.dma_start(kept, a["constants"][:, 0:N_KEPT]).then_inc(const_in, 16)
                sp.dma_start(wz, a["wz"]).then_inc(wz_in, 16)
                sp.dma_start(wab, a["wab"]).then_inc(wz_in, 16)
                sp.dma_start(x_all[:, 2 * DM:].rearrange("p (t d) -> p t d", t=TILES - 2),
                             a["x"][2 * P:, :].rearrange("(t p) d -> p t d", p=P)).then_inc(x_in, 16)
                sp.dma_start(masks, a["constants"][:, N_KEPT:]).then_inc(small_in, 16)
                sp.dma_start(small[:, 0:56], a["per_channel"]).then_inc(small_in, 16)
                sp.dma_start(small[:, 56:64], a["per_head"].partition_broadcast(P)).then_inc(small_in, 16)
                sp.dma_start(out_gain, a["out_gain"].partition_broadcast(P)).then_inc(small_in, 16)
                sp.dma_start(gain_ffn, a["gain_ffn"].partition_broadcast(P)).then_inc(gains_in, 16)
                sp.dma_start(gain_fin, a["gain_fin"].partition_broadcast(P)).then_inc(gains_in, 16)
                for s in range(4):
                    sp.dma_start(wc[s], a["wc"][s, :, :]).then_inc(wc_in[s], 16)

            @block.scalar
            def _(act):
                def root_mean(t):
                    A.activation(junk, x_all[:, ds(t * DM, DM)], ACT.Square, accum_out=stat[:, ds(t, 1)]).then_inc(sq_made, 1)
                    act.wait_ge(ms_made, t + 1)
                    act.sem_inc(scalar_steps, 1)
                    A.activation(stat[:, ds(t + 16, 1)], stat[:, ds(t + 8, 1)], ACT.Sqrt).then_inc(root_made, 1)

                def keep(t, s):
                    act.wait_ge(turned, t + 1)
                    A.activation(hn_tile[s][:, 0:HALF], bank[0], ACT.Copy)
                    A.activation(hn_tile[s][:, HALF:DM], bank[1], ACT.Copy).then_inc(tile_kept, 1)

                def step(t, s, after):
                    if after:
                        act.wait_ge(z_made, t + 0)
                        act.wait_ge(hn_kept, t + 0)
                        keep(t + 1, 1 - s)
                    if after == 2:
                        root_mean(t + 2)
                    act.wait_ge(z_made, t + 1)
                    act.sem_inc(scalar_steps, 1)
                    A.activation(z_all[:, ds(t * HALF, HALF)], bank[2], ACT.Copy)
                    A.activation(ab_all[:, ds(t * 8, 8)], bank[3][:, 0:8], ACT.Copy).then_inc(z_kept, 1)

                act.wait_ge(x_first_in, 16)
                root_mean(0)
                root_mean(1)
                keep(0, 0)
                act.wait_ge(x_in, 16)
                norm_steps(act.Fori, step)

            @block.vector
            def _(dve):
                def mean(t):
                    dve.wait_ge(sq_made, t + 1)
                    V.tensor_scalar(stat[:, ds(t + 8, 1)], stat[:, ds(t, 1)], 1.0 / DM, EPS, ALU.mult, ALU.add).then_inc(ms_made, 1)

                def scale(t):
                    dve.wait_ge(root_made, t + 1)
                    V.reciprocal(stat[:, ds(t + 24, 1)], stat[:, ds(t + 16, 1)]).then_inc(rstd_made, 1)

                def norm(t):
                    dve.wait_ge(rstd_made, t + 1)
                    V.scalar_tensor_tensor(hn, x_all[:, ds(t * DM, DM)], stat[:, ds(t + 24, 1)],
                                           gain_mix, ALU.mult, ALU.mult).then_inc(hn_made, 1)

                def step(t, s, after):
                    if after:
                        dve.wait_ge(turned, t + 1)
                        norm(t + 1)
                    if after == 2:
                        mean(t + 2)
                        scale(t + 2)

                V.memset(eps_col, EPS)
                mean(0)
                scale(0)
                dve.wait_ge(const_in, 32)
                norm(0)
                mean(1)
                scale(1)
                norm_steps(dve.Fori, step)

            @block.tensor
            def _(pe):
                def turn(t):
                    pe.wait_ge(hn_made, t + 1)
                    pe.wait_ge(tile_kept, t + 0)
                    for d in range(DB):
                        m = PE.transpose(bank[d // 4][:, (d % 4) * P:(d % 4 + 1) * P], hn[:, d * P:(d + 1) * P], ident)
                    m.then_inc(turned, 1)

                def step(t, s, after):
                    if after:
                        turn(t + 1)
                    pe.wait_ge(tile_kept, t + 1)
                    pe.wait_ge(z_kept, t + 0)
                    for d in range(DB):
                        PE.matmul(bank[2], hn_tile[s][:, d * P:(d + 1) * P], wz[:, d * HALF:(d + 1) * HALF],
                                  start=(d == 0), stop=(d == DB - 1))
                    for d in range(DB):
                        m = PE.matmul(bank[3][:, 0:8], hn_tile[s][:, d * P:(d + 1) * P], wab[:, d * 8:(d + 1) * 8],
                                      start=(d == 0), stop=(d == DB - 1))
                    m.then_inc(z_made, 1)

                pe.wait_ge(const_in, 32)
                turn(0)
                pe.wait_ge(wz_in, 32)
                norm_steps(pe.Fori, step)

            @block.gpsimd
            def _(pool):
                def step(t, s, after):
                    pool.wait_ge(tile_kept, t + 1)
                    pool.sem_inc(pool_steps, 1)
                    G.tensor_copy(hn_t.rearrange("p (d s) -> p d s", d=DB)[:, :, ds(t * P, P)],
                                  hn_tile[s].rearrange("p (d s) -> p d s", d=DB)).then_inc(hn_kept, 1)

                norm_steps(pool.Fori, step)

        spare, rest = Cut(o_all), Cut(work[:, mix.at:])
        raw = [spare(PAD + SEQ), spare(PAD + SEQ)]
        y = [spare(PAD + SEQ), rest(PAD + SEQ)]
        diff, square, root = rest(SEQ), rest(SEQ), rest(SEQ)
        w_pool = spare(4 * P)
        w_out_in = sem("w_out_in")
        pool_w_in, proj_made, raw_kept, sums_made, silu_made, pooled, pool_kept, pads_made = (
            sem(n) for n in ("pool_w_in", "proj_made", "raw_kept", "sums_made", "silu_made", "pooled", "pool_kept", "pads_made"))
        square_made, square_sum, norm_root, normed = (sem(n) for n in ("square_made", "square_sum", "norm_root", "qk_normed"))

        def qkv_steps(loop, step):
            step(0, 0, None)
            with loop(0, 2) as i:
                for s in range(4):
                    step(i * 4 + (s + 1), (s + 1) % 4, i)
            for u in range(9, 12):
                step(u, u % 4, None)

        with nc.Block() as block:
            @block.sync
            def _(sp):
                sp.dma_start(w_pool, a["w_pool"]).then_inc(pool_w_in, 16)
                with sp.Fori(0, 3) as i:
                    for s in range(4):
                        sp.wait_ge(proj_made, i * 8 + (2 * s + 2))
                        sp.dma_start(wc[s], a["wc"][ds(i * 4 + (4 + s), 1), :, :].rearrange("a p c -> p (a c)")).then_inc(wc_in[s], 16)
                sp.dma_start(w_out, a["w_out"]).then_inc(w_out_in, 16)

            @block.tensor
            def _(pe):
                def project(s, loaded, before):
                    pe.wait_ge(wc_in[s], loaded)
                    for half in range(2):
                        if before is not None:
                            pe.wait_ge(raw_kept, before + half)
                        for d in range(DB):
                            m = PE.matmul(bank[2 * (s % 2) + half], wc[s][:, d * P:(d + 1) * P],
                                          hn_t[:, d * SEQ + half * HALF:d * SEQ + (half + 1) * HALF],
                                          start=(d == 0), stop=(d == DB - 1))
                        m.then_inc(proj_made, 1)

                def pool_product(g):
                    pe.wait_ge(sums_made, g + 1)
                    if g > 0:
                        pe.wait_ge(pool_kept, 2 * g)
                    for half in range(2):
                        PE.matmul(bank[4 + half], w_pool[:, g * P:(g + 1) * P], diff[:, half * HALF:(half + 1) * HALF],
                                  start=True, stop=True).then_inc(pooled, 1)

                project(0, 16, None)
                project(1, 16, None)
                pe.wait_ge(pool_w_in, 16)
                pool_product(0)
                project(2, 16, 1)
                pool_product(1)
                project(3, 16, 3)
                pool_product(2)
                def step(u, s, i):
                    loaded = 16 * (u // 4 + 2) if i is None else i * 16 + (32 if s else 48)
                    project(s, loaded, u * 2 + 5)
                    if isinstance(u, int) and u == 0:
                        pool_product(3)
                    if i is not None:
                        pe.wait_ge(square_made, u)
                        pe.wait_ge(norm_root, u - 1)
                        for half in range(2):
                            m = PE.matmul(bank[6 + half], ones, square[:, half * HALF:(half + 1) * HALF], start=True, stop=True)
                        m.then_inc(square_sum, 1)

                qkv_steps(pe.Fori, step)

            @block.scalar
            def _(act):
                def keep_raw(s, made, read):
                    for half in range(2):
                        act.wait_ge(proj_made, made + half)
                        if half == 0 and read is not None:
                            act.wait_ge(sums_made, read)
                        A.activation(raw[s % 2][:, PAD + half * HALF:PAD + (half + 1) * HALF],
                                     bank[2 * (s % 2) + half], ACT.Copy).then_inc(raw_kept, 1)

                act.wait_ge(pads_made, 1)
                for s in range(4):
                    keep_raw(s, 2 * s + 1, s - 1 if s >= 2 else None)

                def step(u, s, i):
                    keep_raw(s, u * 2 + 9, u + 3)
                    if i is not None:
                        act.wait_ge(square_sum, u + 0)
                        act.wait_ge(normed, u - 1)
                        for half in range(2):
                            m = A.activation(root[:, half * HALF:(half + 1) * HALF], bank[6 + half], ACT.Sqrt, bias=eps_col)
                        m.then_inc(norm_root, 1)
                    act.wait_ge(sums_made, u + 5)
                    at = qkv_t[:, ds(u * SEQ, SEQ)]
                    A.activation(at, y[s % 2][:, PAD:], ACT.Silu).then_inc(silu_made, 1)
                    if isinstance(u, int) and u > 8:
                        return
                    act.wait_ge(silu_made, u + 1)
                    act.wait_ge(square_sum, u + 0)
                    act.sem_inc(scalar_steps, 1)
                    A.activation(square, at, ACT.Square).then_inc(square_made, 1)

                qkv_steps(act.Fori, step)

            @block.vector
            def _(dve):
                def pool_out(g):
                    for half in range(2):
                        dve.wait_ge(pooled, 2 * g + half + 1)
                        V.tensor_scalar(pool_t[:, g * SEQ + half * HALF:g * SEQ + (half + 1) * HALF], bank[4 + half],
                                        b_pool[:, g:g + 1], pool_scale[:, g:g + 1], ALU.add, ALU.mult).then_inc(pool_kept, 1)

                dve.wait_ge(pads_made, 1)
                dve.wait_ge(small_in, 64)
                for g, window in enumerate(POOL_WINDOWS):
                    dve.wait_ge(raw_kept, 2 * g + 2)
                    src, reach, n = raw[g % 2], 1, 0
                    while reach < window:
                        dst = y[n % 2]
                        vc.link(V.tensor_tensor(dst[:, PAD:], src[:, PAD:], src[:, PAD - reach:PAD + SEQ - reach], ALU.add))
                        src, reach, n = dst, 2 * reach, n + 1
                    if g > 0:
                        dve.wait_ge(pooled, 2 * g)
                    vc.link(V.scalar_tensor_tensor(diff, src[:, PAD:], 1.0 / window, raw[g % 2][:, PAD:], ALU.mult, ALU.subtract))
                    vc.link(V.tensor_tensor(diff[:, 0:PAD], src[:, PAD:2 * PAD], inv_count[:, g * PAD:(g + 1) * PAD], ALU.mult))
                    V.tensor_tensor(diff[:, 0:PAD], diff[:, 0:PAD], raw[g % 2][:, PAD:2 * PAD], ALU.subtract).then_inc(sums_made, 1)
                    dve.wait_ge(sums_made, g + 1)
                    if g > 0:
                        pool_out(g - 1)
                pool_out(3)

                def step(u, s, i):
                    dve.wait_ge(raw_kept, u * 2 + 10)
                    dst = y[s % 2][:, PAD:]
                    taps = [small[:, ds(u * 4 + k, 1)] for k in range(TAPS)]
                    if not (isinstance(u, int) and u == 0):
                        dve.wait_ge(silu_made, u - 1)
                    vc.link(V.tensor_scalar(dst, raw[s % 2][:, PAD:], taps[TAPS - 1], None, ALU.mult))
                    for k in range(1, TAPS):
                        m = V.scalar_tensor_tensor(dst, raw[s % 2][:, PAD - k:PAD + SEQ - k], taps[TAPS - 1 - k], dst, ALU.mult, ALU.add)
                        if k < TAPS - 1:
                            vc.link(m)
                        else:
                            m.then_inc(sums_made, 1)
                            dve.wait_ge(sums_made, u + 5)
                    if i is not None:
                        dve.wait_ge(norm_root, u + 0)
                        vc.link(V.reciprocal(root, root))
                        at = qkv_t[:, ds(u * SEQ - SEQ, SEQ)]
                        V.tensor_tensor(at, at, root, ALU.mult).then_inc(normed, 1)

                qkv_steps(lambda first, end: vc.loop(first, end, 4 * TAPS), step)

            @block.gpsimd
            def _(pool):
                for buf in (raw[0], raw[1], y[0]):
                    G.memset(buf[:, 0:PAD], 0.0)
                G.memset(y[1][:, 0:PAD], 0.0).then_inc(pads_made, 1)

        TH = TILES * HEADS
        cut = Cut(work[:, mix.at:])
        log_dec, log_sum, beta, beta_dec, dec_end, sp_a, sp_b, sp_c = (cut(TH) for _ in range(8))
        exp_sum = sp_a
        b_raw = ab_all.rearrange("p (t c) -> p t c", t=TILES)[:, :, 0:HEADS]
        a_raw = ab_all.rearrange("p (t c) -> p t c", t=TILES)[:, :, HEADS:2 * HEADS]

        def by_tile(ap):
            return ap.rearrange("p (t h) -> p t h", t=TILES)

        def over_tiles(ap):
            return ap.unsqueeze(1).to_broadcast([P, TILES, HEADS])

        soft_in, soft_e, soft_l, dec_made, sums_done, exps_done = (
            sem(n) for n in ("softplus_in", "softplus_exp", "softplus_log", "log_decay_made", "decay_sums_made", "decay_exps_made"))
        with nc.Block() as block:
            @block.vector
            def _(dve):
                vc.link(V.tensor_tensor(by_tile(sp_a), a_raw, over_tiles(dt_bias), ALU.add))
                vc.link(V.tensor_scalar(sp_b, sp_a, -1.0, None, ALU.mult))
                V.tensor_tensor(sp_b, sp_b, sp_a, ALU.min).then_inc(soft_in, 1)
                dve.wait_ge(soft_e, 3)
                vc.link(V.tensor_scalar(beta, beta, 1.0, None, ALU.add))
                vc.link(V.reciprocal(beta, beta))
                dve.wait_ge(soft_l, 1)
                vc.link(V.scalar_tensor_tensor(sp_c, sp_a, 0.0, sp_c, ALU.max, ALU.add))
                V.scalar_tensor_tensor(by_tile(log_dec), by_tile(sp_c), -1.0, over_tiles(stat[:, 0:HEADS]), ALU.mult, ALU.mult).then_inc(dec_made, 1)
                dve.wait_ge(exps_done, 1)
                vc.link(V.tensor_copy(log_sum, bank[0][:, 0:TH]))
                vc.link(V.tensor_tensor(beta_dec, beta, exp_sum, ALU.mult))

            @block.scalar
            def _(act):
                A.activation(stat[:, 0:HEADS], a_log, ACT.Exp).then_inc(soft_e, 1)
                A.activation(by_tile(beta), b_raw, ACT.Exp, scale=-1.0).then_inc(soft_e, 1)
                act.wait_ge(soft_in, 1)
                A.activation(sp_b, sp_b, ACT.Exp).then_inc(soft_e, 1)
                act.wait_ge(soft_e, 3)
                A.activation(sp_c, sp_b, ACT.Ln, bias=1.0).then_inc(soft_l, 1)
                act.wait_ge(sums_done, 1)
                A.activation(exp_sum, bank[0][:, 0:TH], ACT.Exp)
                A.activation(dec_end, bank[0][:, TH:2 * TH], ACT.Exp).then_inc(exps_done, 1)

            @block.tensor
            def _(pe):
                pe.wait_ge(dec_made, 1)
                PE.matmul(bank[0][:, 0:TH], causal, log_dec, start=True, stop=True)
                PE.matmul(bank[0][:, TH:2 * TH], after, log_dec, start=True, stop=True).then_inc(sums_done, 1)

        pieces = [hn_t[:, n * HALF:(n + 1) * HALF] for n in range(16)]
        pieces += [late[:, 12 * SEQ + n * HALF:12 * SEQ + (n + 1) * HALF] for n in range(8)]
        pieces += [cut(HALF) for _ in range(6)]
        (sum_rhs, beta_rhs, k_tile, v_tile, dec, row_dec, solve, inv, inv_t, prod, u_tile, w_tile, v_new, state, middle) = pieces[:15]
        lower = pieces[15:20]
        k_beta, v_beta = k_tile, v_tile
        scores, q_first, q_second, k_first, k_second = (pieces[20 + 2 * n:22 + 2 * n] for n in range(5))
        ends = [cut(2 * HEADS) for _ in range(2)]
        q_all, k_all, v_all = (qkv_t[:, n * 4 * SEQ:(n + 1) * 4 * SEQ].rearrange("p (h s) -> p h s", h=HEADS) for n in range(3))
        names = ("zeroed", "kv_kept", "sum_rhs_made", "beta_rhs_made", "rows_made", "kk_made", "turned_kv", "diff_made", "dec_exp", "rows_exp",
                 "solve_made", "lower_made", "inv_t_made", "inv_turned", "inv_made", "prod_made", "prod_kept", "corr_made",
                 "corr_t_made", "inv_done", "level_done", "keys_taken", "uw_made", "uw_kept", "ws_made", "v_new_made", "gain_made",
                 "state_made", "o_made", "o_kept")
        S = {n: sem("d_" + n) for n in names}
        NL, Q_SCALE = len(LEVELS), HD ** -0.5

        def in_pairs(loop, tile):
            tile(0, 0, False)
            tile(1, 1, True)
            with loop(1, TILES // 2) as i:
                for s in range(2):
                    tile(i * 2 + s, s, True)

        with nc.Block() as block:
            @block.gpsimd
            def _(pool):
                with pool.Fori(0, TILES) as t:
                    pool.wait_ge(S["rows_made"], t)
                    pool.sem_inc(pool_steps, 1)
                    four = ds(t * HEADS, HEADS)
                    G.tensor_tensor(per_head(sum_rhs), over_heads(causal), over_cols(log_dec[:, four]), ALU.mult).then_inc(S["sum_rhs_made"], 1)
                    G.tensor_tensor(per_head(beta_rhs), over_heads(ident), over_cols(beta[:, four]), ALU.mult).then_inc(S["beta_rhs_made"], 1)
                    pool.wait_ge(S["solve_made"], t + 1)
                    pool.wait_ge(S["level_done"], t * NL)
                    for n in range(NL):
                        G.tensor_tensor(per_head(lower[n]), per_head(solve), over_heads(level_mask[n + 1]), ALU.mult).then_inc(S["lower_made"], 1)

            @block.scalar
            def _(act):
                def output(t):
                    act.wait_ge(S["o_made"], t + 1)
                    A.activation(o_all[:, ds(t * HALF, HALF)], bank[4], ACT.Copy)
                    act.wait_ge(S["state_made"], t * 2 + 2)
                    for h in range(HEADS):
                        cols = slice(h * P, (h + 1) * P)
                        m = A.activation(w_tile[:, cols], bank[4][:, cols], ACT.Square, accum_out=o_stat[:, ds(t * HEADS + h, 1)])
                    m.then_inc(S["o_kept"], 1)
                    act.wait_ge(S["o_kept"], t + 1)

                def tile(t, s, before):
                    act.wait_ge(S["uw_made"], t + 0)
                    A.activation(per_head(k_tile), k_all[:, :, ds(t * P, P)], ACT.Copy)
                    A.activation(per_head(v_tile), v_all[:, :, ds(t * P, P)], ACT.Copy).then_inc(S["kv_kept"], 1)
                    act.wait_ge(S["diff_made"], t + 1)
                    A.activation(dec, dec, ACT.Exp).then_inc(S["dec_exp"], 1)
                    A.activation(row_dec, bank[0], ACT.Exp).then_inc(S["rows_exp"], 1)
                    act.wait_ge(S["inv_turned"], t + 1)
                    A.activation(inv, bank[6], ACT.Copy).then_inc(S["inv_made"], 1)
                    for n in range(NL):
                        act.wait_ge(S["prod_made"], t * NL + (n + 1))
                        A.activation(prod, bank[6], ACT.Copy).then_inc(S["prod_kept"], 1)
                    if before:
                        output(t - 1)
                    act.wait_ge(S["uw_made"], t + 1)
                    A.activation(u_tile, bank[2], ACT.Copy)
                    A.activation(w_tile, bank[3], ACT.Copy).then_inc(S["uw_kept"], 1)

                in_pairs(act.Fori, tile)
                output(TILES - 1)

            @block.vector
            def _(dve):
                def tokens(n, t, s):
                    four = ds(t * HEADS, HEADS)
                    if n == 0:
                        dve.wait_ge(S["turned_kv"], t + 1)
                        V.tensor_tensor(per_head(v_beta), per_head(bank[5]), over_cols(beta[:, four]), ALU.mult)
                        V.tensor_tensor(per_head(k_beta), per_head(bank[4]), over_cols(beta_dec[:, four]), ALU.mult)
                    elif n < 3:
                        of = slice((n - 1) * CHUNK, n * CHUNK)
                        m = V.tensor_tensor(per_head((k_first, k_second)[n - 1][s])[of], per_head(bank[4])[of], over_cols(dec_end[of, four]), ALU.mult)
                        if n == 2:
                            m.then_inc(S["keys_taken"], 1)
                    else:
                        c = n - 3
                        if c == 0:
                            dve.wait_ge(S["rows_exp"], t + 1)
                            V.tensor_copy(ends[s].rearrange("p (h c) -> p h c", h=HEADS),
                                          row_dec.rearrange("p (h c k) -> p h c k", h=HEADS, c=2)[:, :, :, CHUNK - 1])
                        of = slice(c * CHUNK, (c + 1) * CHUNK)
                        V.scalar_tensor_tensor(per_head((q_first, q_second)[c][s])[:, :, of], q_all[:, :, ds(t * P + c * CHUNK, CHUNK)],
                                               Q_SCALE, per_head(row_dec)[:, :, of], ALU.mult, ALU.mult)

                def take(c, t):
                    of = slice(c * CHUNK, (c + 1) * CHUNK)
                    dve.wait_ge(S["ws_made"], t * 2 + (c + 1))
                    V.tensor_tensor(v_new[of], u_tile[of], bank[1][of], ALU.subtract).then_inc(S["v_new_made"], 1)

                def carry(c, t, s):
                    old, new = ((state, middle), (middle, state))[c]
                    dve.wait_ge(S["gain_made"], t * 2 + (c + 1))
                    if c == 1:
                        dve.wait_ge(S["o_made"], t + 1)
                    for h in range(HEADS):
                        cols = slice(h * P, (h + 1) * P)
                        m = V.scalar_tensor_tensor(new[:, cols], old[:, cols], ends[s][:, 2 * h + c:2 * h + c + 1],
                                                   bank[5][:, cols], ALU.mult, ALU.add)
                    m.then_inc(S["state_made"], 1)
                    dve.wait_ge(S["state_made"], t * 2 + (c + 1))

                def state_step(n, t, s):
                    if n in (0, 2):
                        take(n // 2, t)
                    elif n == 1:
                        carry(0, t, s)
                    elif n == 4:
                        carry(1, t, s)

                def tile(t, s, before):
                    four = ds(t * HEADS, HEADS)
                    dve.wait_ge(S["rows_made"], t + 1)
                    vc.link(V.tensor_tensor(per_head(dec), per_head(bank[0]), over_cols(log_sum[:, four]), ALU.subtract))
                    V.tensor_tensor(per_head(dec), per_head(dec), over_heads(causal), ALU.mult).then_inc(S["diff_made"], 1)
                    dve.wait_ge(S["dec_exp"], t + 1)
                    vc.link(V.tensor_tensor(per_head(dec), per_head(dec), over_heads(causal), ALU.mult))
                    dve.wait_ge(S["kk_made"], t + 1)
                    dve.wait_ge(S["lower_made"], t * NL)
                    vc.link(V.tensor_tensor(solve, bank[2], dec, ALU.mult))
                    V.tensor_tensor(solve, solve, bank[1], ALU.mult).then_inc(S["solve_made"], 1)
                    V.scalar_tensor_tensor(scores[s], bank[3], Q_SCALE, dec, ALU.mult, ALU.mult)
                    dve.wait_ge(S["solve_made"], t + 1)
                    vc.link(V.tensor_tensor(per_head(inv_t), per_head(solve), over_heads(level_mask[0]), ALU.mult))
                    V.tensor_tensor(per_head(inv_t), over_heads(ident), per_head(inv_t), ALU.subtract).then_inc(S["inv_t_made"], 1)
                    dve.wait_ge(S["inv_made"], t + 1)
                    for n in range(NL):
                        if n < NL - 1:
                            dve.wait_ge(S["corr_made"], t * (NL - 1) + (n + 1))
                            V.tensor_tensor(inv, inv, bank[7], ALU.subtract).then_inc(S["inv_done"], 1)
                        dve.wait_ge(S["corr_t_made"], t * NL + (n + 1))
                        V.tensor_tensor(inv_t, inv_t, bank[0], ALU.subtract).then_inc(S["level_done"], 1)
                        tokens(n, t, s)
                        if before:
                            state_step(n, t - 1, 1 - s)
                        dve.wait_ge(S["level_done"], t * NL + (n + 1))

                for buf in [state, v_new] + q_first + q_second + k_first:
                    V.memset(buf, 0.0)
                for buf in k_second:
                    V.memset(buf, 0.0).then_inc(S["zeroed"], 1)
                dve.wait_ge(S["zeroed"], 2)
                in_pairs(lambda first, end: vc.loop(first, end, 2 * 4), tile)
                dve.wait_ge(S["uw_kept"], TILES)
                for n in range(NL):
                    state_step(n, TILES - 1, 1)

            @block.tensor
            def _(pe):
                def heads(to, left, right):
                    for h in range(HEADS):
                        c = slice(h * P, (h + 1) * P)
                        m = PE.matmul(to[:, c], left[:, c], right[:, c], start=True, stop=True)
                    return m

                def turn(to, of):
                    for h in range(HEADS):
                        c = slice(h * P, (h + 1) * P)
                        m = PE.transpose(to[:, c], of[:, c], ident)
                    return m

                def state_step(n, t, s):
                    if n == 0:
                        pe.wait_ge(S["uw_kept"], t + 1)
                        pe.wait_ge(S["state_made"], t * 2)
                    if n == 2:
                        pe.wait_ge(S["state_made"], t * 2 + 1)
                    if n in (0, 2):
                        heads(bank[1], w_tile, (state, middle)[n // 2]).then_inc(S["ws_made"], 1)
                    elif n in (1, 3):
                        pe.wait_ge(S["v_new_made"], t * 2 + (n // 2 + 1))
                        heads(bank[5], (k_first, k_second)[n // 2][s], v_new).then_inc(S["gain_made"], 1)
                    else:
                        for h in range(HEADS):
                            c = slice(h * P, (h + 1) * P)
                            PE.matmul(bank[4][:, c], q_first[s][:, c], state[:, c], start=True, stop=False)
                            PE.matmul(bank[4][:, c], q_second[s][:, c], middle[:, c], start=False, stop=False)
                            m = PE.matmul(bank[4][:, c], scores[s][:, c], v_new[:, c], start=False, stop=True)
                        m.then_inc(S["o_made"], 1)

                def tile(t, s, before):
                    pe.wait_ge(S["sum_rhs_made"], t + 1)
                    pe.wait_ge(S["beta_rhs_made"], t + 1)
                    PE.matmul(bank[0], ones, sum_rhs, start=True, stop=True)
                    PE.matmul(bank[1], ones, beta_rhs, start=True, stop=True).then_inc(S["rows_made"], 1)
                    pe.wait_ge(S["kv_kept"], t + 1)
                    heads(bank[2], k_tile, k_tile)
                    for h in range(HEADS):
                        c = slice(h * P, (h + 1) * P)
                        m = PE.matmul(bank[3][:, c], k_tile[:, c], q_all[:, h, ds(t * P, P)], start=True, stop=True)
                    m.then_inc(S["kk_made"], 1)
                    turn(bank[4], k_tile)
                    turn(bank[5], v_tile).then_inc(S["turned_kv"], 1)
                    pe.wait_ge(S["inv_t_made"], t + 1)
                    turn(bank[6], inv_t).then_inc(S["inv_turned"], 1)
                    pe.wait_ge(S["inv_made"], t + 1)
                    for n in range(NL):
                        pe.wait_ge(S["lower_made"], t * NL + (n + 1))
                        if n > 0:
                            pe.wait_ge(S["inv_done"], t * (NL - 1) + n)
                        heads(bank[6], lower[n], inv).then_inc(S["prod_made"], 1)
                        if before:
                            if n == NL - 1:
                                pe.wait_ge(S["keys_taken"], t + 1)
                            state_step(n, t - 1, 1 - s)
                        pe.wait_ge(S["prod_kept"], t * NL + (n + 1))
                        pe.wait_ge(S["level_done"], t * NL + n)
                        if n < NL - 1:
                            heads(bank[7], inv_t, prod).then_inc(S["corr_made"], 1)
                        heads(bank[0], prod, inv_t).then_inc(S["corr_t_made"], 1)
                    pe.wait_ge(S["level_done"], t * NL + NL)
                    pe.wait_ge(S["keys_taken"], t + 1)
                    heads(bank[2], inv_t, v_beta)
                    heads(bank[3], k_beta, inv_t).then_inc(S["uw_made"], 1)

                pe.wait_ge(S["zeroed"], 2)
                in_pairs(pe.Fori, tile)
                for n in range(NL):
                    state_step(n, TILES - 1, 1)

        cut = Cut(work[:, mix.at:])
        gated = cut(HALF)
        w_query = [cut(DM + NKEYS) for _ in range(2)]
        w_query_in = [sem(f"w_query_in{n}") for n in range(2)]
        mixed_out, x_tile_in = sem("mixed_out"), sem("x_tile_in")
        h_next = work[:, 0:DM]
        HEADS_FIRST = 3
        mixed_tiles = nc.dram_tensor("mixed_tiles", (TILES, P, DM), F32).ap()
        names = ("key_product", "w_score_kept", "means", "roots", "rstds", "z_silu", "gated", "turned", "turned_kept", "pool_stored", "stored")
        M = {n: sem("m_" + n) for n in names}

        def weight_product(queries, keys, banks):
            for d in range(DB):
                m = PE.matmul(banks[d // 4][:, (d % 4) * P:(d % 4 + 1) * P], queries[:, d * P:(d + 1) * P], keys, start=True, stop=True)
            m.then_inc(M["key_product"], 1)

        def keep_weights(j, s, banks):
            to = w_score.rearrange("p (d k) -> p d k", d=DB)[:, :, ds(j * QD + s * P, P)]
            for n in range(2):
                m = A.activation(to[:, 4 * n:4 * n + 4, :], banks[n].rearrange("p (d k) -> p d k", d=4), ACT.Copy)
            m.then_inc(M["w_score_kept"], 1)

        with nc.Block() as block:
            @block.sync
            def _(sp):
                sp.dma_start(h_next, a["x"][0:P, :]).then_inc(x_tile_in, 16)
                for s in range(2):
                    sp.dma_start(w_query[s], a["w_query"][s, :, :]).then_inc(w_query_in[s], 16)
                for g in range(4):
                    sp.dma_start(mixed_tiles[:, :, g * P:(g + 1) * P].rearrange("t p k -> p t k"),
                                 pool_t[:, g * SEQ:(g + 1) * SEQ].rearrange("p (t k) -> p t k", t=TILES)).then_inc(M["pool_stored"], 16)
                with sp.Fori(0, HEADS_FIRST - 1) as i:
                    for s in range(2):
                        sp.wait_ge(M["key_product"], i * 2 + (s + 1))
                        sp.dma_start(w_query[s], a["w_query"][ds(i * 2 + (s + 2), 1), :, :].rearrange("a p c -> p (a c)")).then_inc(w_query_in[s], 16)
                sp.wait_ge(M["turned_kept"], TILES)
                sp.dma_start(mixed_tiles[:, :, HALF:].rearrange("t p k -> p t k"),
                             z_all.rearrange("p (t k) -> p t k", t=TILES)).then_inc(M["stored"], 16)
                sp.wait_ge(M["pool_stored"], 16 * 4)

            @block.scalar
            def _(act):
                act.wait_ge(M["means"], 1)
                A.activation(o_stat[:, TH:2 * TH], o_stat[:, 0:TH], ACT.Sqrt).then_inc(M["roots"], 1)
                A.activation(z_all, z_all, ACT.Silu).then_inc(M["z_silu"], 1)

                def keep_turned(t):
                    act.wait_ge(M["turned"], t + 1)
                    act.sem_inc(scalar_steps, 1)
                    A.activation(z_all[:, ds(t * HALF, HALF)], bank[2], ACT.Copy).then_inc(M["turned_kept"], 1)

                with act.Fori(0, HEADS_FIRST) as t:
                    for s in range(2):
                        act.wait_ge(M["key_product"], t * 2 + (s + 1))
                        act.sem_inc(scalar_steps, 1)
                        keep_weights(t, s, bank[4 + 2 * s:6 + 2 * s])
                    keep_turned(t)
                with act.Fori(HEADS_FIRST, TILES) as t:
                    keep_turned(t)

            @block.vector
            def _(dve):
                V.tensor_scalar(o_stat[:, 0:TH], o_stat[:, 0:TH], 1.0 / HD, EPS, ALU.mult, ALU.add).then_inc(M["means"], 1)
                dve.wait_ge(M["roots"], 1)
                V.reciprocal(o_stat[:, 2 * TH:3 * TH], o_stat[:, TH:2 * TH]).then_inc(M["rstds"], 1)
                dve.wait_ge(M["rstds"], 1)
                with vc.loop(0, TILES, 2) as t:
                    dve.wait_ge(M["turned"], t + 0)
                    vc.link(V.tensor_tensor(per_head(gated), per_head(o_all[:, ds(t * HALF, HALF)]), over_cols(o_stat[:, ds(t * HEADS + 2 * TH, HEADS)]), ALU.mult))
                    vc.link(V.tensor_tensor(per_head(gated), per_head(gated), over_heads(out_gain), ALU.mult))
                    dve.wait_ge(M["z_silu"], 1)
                    V.tensor_tensor(gated, gated, z_all[:, ds(t * HALF, HALF)], ALU.mult).then_inc(M["gated"], 1)

            @block.tensor
            def _(pe):
                def turn(t):
                    pe.wait_ge(M["gated"], t + 1)
                    pe.wait_ge(M["turned_kept"], t + 0)
                    for h in range(HEADS):
                        c = slice(h * P, (h + 1) * P)
                        m = PE.transpose(bank[2][:, c], gated[:, c], ident)
                    m.then_inc(M["turned"], 1)

                with pe.Fori(0, HEADS_FIRST) as t:
                    for s in range(2):
                        pe.wait_ge(w_query_in[s], t * 16 + 16)
                        pe.wait_ge(M["w_score_kept"], t * 2)
                        weight_product(w_query[s][:, 0:DM], w_query[s][:, DM:], bank[4 + 2 * s:6 + 2 * s])
                    turn(t)
                pe.wait_ge(w_out_in, 16)
                pe.wait_ge(M["w_score_kept"], HEADS_FIRST * 2)
                every = 2 * DB // (TILES - HEADS_FIRST)
                for n in range(2 * DB):
                    half, d = n // DB, n % DB
                    src = pool_t[:, d * SEQ:d * SEQ + P] if d < 4 else z_all[:, (d - 4) * P:(d - 3) * P]
                    m = PE.matmul(bank[3 + half], src, w_out[:, d * DM + half * HALF:d * DM + (half + 1) * HALF],
                                  start=(d == 0), stop=(d == DB - 1))
                    if n == 2 * DB - 1:
                        m.then_inc(mixed_out, 1)
                    if n % every == every - 1:
                        turn(HEADS_FIRST + n // every)

        cut = Cut(work)
        cut(DM)
        h_now, hf_now, hf_next, hf_t = (cut(DM) for _ in range(4))
        mixed, out_tile = cut(DM), cut(DM)
        some_queries, some_keys = out_tile, cut(NKEYS)
        some_in = sem("some_queries_in")
        diag = [cut(P) for _ in range(RING)]
        picks = cut(PICKS).bitcast(I32)
        pick_now = cut(TOPK).bitcast(I32)
        gates, gate_sum, gate_scale = cut(PICKS), cut(PHEADS), cut(PHEADS)
        val, ix, ix_f = cut(2 * TOPK), cut(2 * TOPK).bitcast(U32), cut(2 * TOPK)
        same = cut(2 * TOPK * TOPK)
        left, pairs = same[:, 0:2 * P], same[:, 2 * P:4 * P]
        pos, pos_hl, pos_f = cut(TOPK).bitcast(U32), cut(2 * TOPK).bitcast(U32), cut(2 * TOPK)
        found = cut(2 * TOPK)
        dots, scored_gelu, weights = cut(TOPK), cut(TOPK), cut(TOPK)
        f_stat, n_stat = stat[:, 0:4], stat[:, 4:8]
        ring = [ring_mem[:, n * 2 * DM:(n + 1) * 2 * DM] for n in range(RING)]
        names = ("hf_made", "hf_turned", "hf_kept", "scored", "picked", "gates_made", "used", "dot_made", "gelu_made",
                 "weights_made", "diag_made", "summed", "f_sumsq", "f_mean", "f_root", "out_made", "out_stored", "picks_now",
                 "mixed_in", "h_made", "h_moved", "n_sumsq", "n_mean", "n_root")
        X = {n: sem("x_" + n) for n in names}
        got = [sem(f"got{n}") for n in range(RING)]
        USED0 = TOPK
        GROUPS = TOPK // GROUP
        AHEAD = 2
        TURN = PHEADS - AHEAD - 1
        START, END = 0, PHEADS - 1

        def makes_weights(first, j):
            return first and (at(j, START) or not isinstance(j, int))

        def at(j, head):
            return isinstance(j, int) and j == head

        with nc.Block() as block:
            @block.gpsimd
            def _(pool):
                pool.wait_ge(M["stored"], 16)
                with pool.Fori(0, TILES) as t:
                    pool.sem_inc(pool_steps, 1)
                    with pool.Fori(0, PHEADS) as j:
                        pool.wait_ge(X["picked"], t * PHEADS + (j + 1))
                        pool.sem_inc(pool_steps, 1)
                        for half in range(2):
                            pool.wait_ge(X["used"], t * PICKS + j * TOPK + (USED0 - TOPK + 8 * half + 8))
                            pool.sem_inc(pool_steps, 1)
                            G.tensor_copy(pick_now[:, half * 8:half * 8 + 8],
                                          picks[:, ds(j * TOPK + half * 8, 8)]).then_inc(X["picks_now"], 1)
                            pool.wait_ge(X["picks_now"], t * (2 * PHEADS) + j * 2 + (half + 1))
                            pool.sem_inc(pool_steps, 1)
                            for k in range(half * 8, half * 8 + 8):
                                pool.wait_ge(X["used"], t * PICKS + j * TOPK + (USED0 + k - RING + 1))
                                pool.sem_inc(pool_steps, 1)
                                G.indirect_dma_start(ring[k % RING], None, a["experts"],
                                                     bass.IndirectOffsetOnAxis(ap=pick_now[:, k:k + 1], axis=0)).then_inc(got[k % RING], 16)

            @block.sync
            def _(sp):
                def load_mixed(t):
                    sp.dma_start(mixed, mixed_tiles[ds(t, 1), :, :].rearrange("a p k -> p (a k)")).then_inc(X["mixed_in"], 16)

                def load_x(t):
                    sp.dma_start(h_next, a["x"][ds(t * P, P), :]).then_inc(x_tile_in, 16)

                def store(t):
                    sp.wait_ge(X["out_made"], t + 1)
                    sp.dma_start(out[ds(t * P, P), :], out_tile).then_inc(X["out_stored"], 16)

                def load_queries(n):
                    sp.wait_ge(M["key_product"], n)
                    sp.dma_start(some_queries, a["w_query"][n, :, 0:DM]).then_inc(some_in, 16)
                    sp.dma_start(some_keys, a["w_query"][n, :, DM:]).then_inc(some_in, 16)

                sp.wait_ge(M["stored"], 16)
                load_mixed(1)
                load_queries(2 * HEADS_FIRST)
                sp.wait_ge(mixed_out, 2)
                load_mixed(2)
                load_queries(2 * HEADS_FIRST + 1)
                sp.wait_ge(X["h_moved"], 1)
                load_x(1)
                for n in range(2 * HEADS_FIRST + 2, 2 * PHEADS):
                    load_queries(n)
                with sp.Fori(0, TILES - 3) as t:
                    sp.wait_ge(mixed_out, t + 3)
                    load_mixed(t + 3)
                    store(t)
                    sp.wait_ge(X["h_moved"], t + 2)
                    load_x(t + 2)
                store(TILES - 3)
                sp.wait_ge(X["h_moved"], TILES - 1)
                load_x(TILES - 1)
                store(TILES - 2)
                store(TILES - 1)
                sp.wait_ge(X["out_stored"], 16 * TILES)

            @block.scalar
            def _(act):
                def turned(t):
                    act.wait_ge(X["hf_turned"], t + 1)
                    A.activation(hf_t[:, 0:HALF], bank[0], ACT.Copy)
                    A.activation(hf_t[:, HALF:DM], bank[1], ACT.Copy).then_inc(X["hf_kept"], 1)

                def gate(n, j):
                    act.wait_ge(X["picked"], n + 1)
                    part = gates[:, ds(j * TOPK, TOPK)]
                    A.activation(part, part, ACT.Exp, accum_out=gate_sum[:, ds(j, 1)]).then_inc(X["gates_made"], 1)

                def final_sum(t):
                    act.wait_ge(X["summed"], t + 1)
                    act.wait_ge(X["out_stored"], t * 16)
                    A.activation(out_tile, h_now, ACT.Square, accum_out=f_stat[:, 0:1]).then_inc(X["f_sumsq"], 1)

                def final_root(t):
                    act.wait_ge(X["f_mean"], t + 1)
                    A.activation(f_stat[:, 2:3], f_stat[:, 1:2], ACT.Sqrt).then_inc(X["f_root"], 1)

                def next_sum(t):
                    act.wait_ge(X["h_made"], t + 1)
                    A.activation(hf_next, h_next, ACT.Square, accum_out=n_stat[:, 0:1]).then_inc(X["n_sumsq"], 1)

                def next_root(t):
                    act.wait_ge(X["n_mean"], t + 1)
                    A.activation(n_stat[:, 2:3], n_stat[:, 1:2], ACT.Sqrt).then_inc(X["n_root"], 1)

                def step(t, j, first, last, jn):
                    for m in range(GROUPS):
                        of = slice(m * GROUP, (m + 1) * GROUP)
                        act.wait_ge(X["dot_made"], t * PICKS + j * TOPK + (m + 1) * GROUP)
                        A.activation(scored_gelu[:, of], dots[:, of], ACT.Gelu).then_inc(X["gelu_made"], 1)
                        act.wait_ge(X["weights_made"], t * (PHEADS * GROUPS) + j * GROUPS + (m + 1))
                        for k in range(m * GROUP, (m + 1) * GROUP):
                            act.wait_ge(X["used"], t * PICKS + j * TOPK + (USED0 + k - RING + 1))
                            A.activation(diag[k % RING], ident, ACT.Copy, scale=weights[:, k:k + 1]).then_inc(X["diag_made"], 1)
                        if m % 2 == 1 and makes_weights(first, j):
                            act.wait_ge(M["key_product"], j * 2 + (2 * HEADS_FIRST + m // 2 + 1))
                            act.sem_inc(scalar_steps, 1)
                            keep_weights(j + HEADS_FIRST, m // 2, bank[0:2])
                        if m == 1 and jn is not None:
                            gate(t * PHEADS + (j + 1), jn)
                        if at(j, TURN) and not last and m != 2:
                            {0: next_sum, 1: next_root, 3: turned}[m](t + 1)
                        if at(j, START) and not first:
                            if m == 0:
                                final_sum(t - 1)
                            if m == 1:
                                final_root(t - 1)

                def tile(t, first=False, last=False):
                    step(t, START, first, last, 1)
                    with act.Fori(1, TURN) as j:
                        step(t, j, first, last, j + 1)
                    for j in range(TURN, PHEADS - 1):
                        step(t, j, first, last, j + 1)
                    step(t, PHEADS - 1, first, last, None if last else 0)

                next_sum(0)
                next_root(0)
                turned(0)
                gate(0, 0)
                tile(0, first=True)
                with act.Fori(1, TILES - 1) as t:
                    tile(t)
                tile(TILES - 1, last=True)
                final_sum(TILES - 1)
                final_root(TILES - 1)

            @block.vector
            def _(dve):
                def link_held(instruction):
                    vc.link(instruction)
                    V.sem_inc(vector_steps, 1)

                def residual(t):
                    dve.wait_ge(x_tile_in, t * 16 + 16)
                    dve.wait_ge(mixed_out, t + 1)
                    for half in range(2):
                        h = h_next[:, half * HALF:(half + 1) * HALF]
                        m = V.tensor_tensor(h, bank[3 + half], h, ALU.add)
                    m.then_inc(X["h_made"], 1)

                def next_mean(t):
                    dve.wait_ge(X["n_sumsq"], t + 1)
                    V.tensor_scalar(n_stat[:, 1:2], n_stat[:, 0:1], 1.0 / DM, EPS, ALU.mult, ALU.add).then_inc(X["n_mean"], 1)

                def query(t):
                    dve.wait_ge(X["n_root"], t + 1)
                    vc.link(V.reciprocal(n_stat[:, 3:4], n_stat[:, 2:3]))
                    V.scalar_tensor_tensor(hf_next, h_next, n_stat[:, 3:4], gain_ffn, ALU.mult, ALU.mult).then_inc(X["hf_made"], 1)

                def move(t):
                    V.tensor_copy(h_now, h_next).then_inc(X["h_moved"], 1)

                def top16(values, indices, src, rest):
                    link_held(V.max(values[:, 0:8], src))
                    V.max_index(indices[:, 0:8], values[:, 0:8], src)
                    link_held(V.match_replace(rest, values[:, 0:8], src, LOW))
                    link_held(V.max(values[:, 8:16], rest))
                    link_held(V.max_index(indices[:, 8:16], values[:, 8:16], rest))

                def pick(piece, t, j, jp):
                    n = t * PHEADS + (j + AHEAD)
                    if piece < 2:
                        of = slice(piece * TOPK, (piece + 1) * TOPK)
                        if piece == 0:
                            dve.wait_ge(X["scored"], n + 1)
                            V.sem_inc(vector_steps, 1)
                        top16(val[:, of], ix[:, of], bank[2][:, piece * P:(piece + 1) * P], left[:, 0:P])
                    elif piece == 2:
                        link_held(V.tensor_tensor(pairs.rearrange("p (i k) -> p i k", i=TOPK),
                                                  val[:, 0:TOPK].unsqueeze(2).to_broadcast([P, TOPK, TOPK]),
                                                  val[:, TOPK:].unsqueeze(1).to_broadcast([P, TOPK, TOPK]), ALU.add))
                        top16(val[:, 0:TOPK], pos, pairs, left)
                    else:
                        V.tensor_scalar(gates[:, ds(jp * TOPK, TOPK)], val[:, 0:TOPK], val[:, 0:1], None, ALU.subtract)
                        V.tensor_copy(ix_f, ix)
                        V.tensor_scalar(pos_hl[:, 0:TOPK], pos, 4, None, ALU.logical_shift_right)
                        vc.link(V.tensor_scalar(pos_hl[:, TOPK:], pos, TOPK - 1, None, ALU.bitwise_and))
                        vc.link(V.tensor_copy(pos_f, pos_hl))
                        three = same.rearrange("p (k i) -> p k i", i=TOPK)
                        vc.link(V.tensor_tensor(three, pos_f.unsqueeze(2).to_broadcast([P, 2 * TOPK, TOPK]),
                                                iota.unsqueeze(1).to_broadcast([P, 2 * TOPK, TOPK]), ALU.is_equal))
                        for h in range(2):
                            part = three[:, h * TOPK:(h + 1) * TOPK, :]
                            m = V.tensor_tensor(part, part, ix_f[:, h * TOPK:(h + 1) * TOPK].unsqueeze(1).to_broadcast([P, TOPK, TOPK]), ALU.mult)
                        vc.link(m)
                        vc.link(V.tensor_reduce(found, three, AX.X, ALU.add))
                        V.scalar_tensor_tensor(picks[:, ds(jp * TOPK, TOPK)], found[:, 0:TOPK], float(NKEYS),
                                               found[:, TOPK:], ALU.mult, ALU.add).then_inc(X["picked"], 1)
                        dve.wait_ge(X["picked"], n + 1)

                def gate(n, j):
                    dve.wait_ge(X["gates_made"], n + 1)
                    vc.link(V.reciprocal(gate_scale[:, ds(j, 1)], gate_sum[:, ds(j, 1)]))

                def take_sum(t):
                    dve.wait_ge(X["used"], t * PICKS + (USED0 + PICKS))
                    for half in range(2):
                        h = h_now[:, half * HALF:(half + 1) * HALF]
                        m = V.tensor_tensor(h, bank[6 + half], h, ALU.add)
                    m.then_inc(X["summed"], 1)

                def final_mean(t):
                    dve.wait_ge(X["f_sumsq"], t + 1)
                    V.tensor_scalar(f_stat[:, 1:2], f_stat[:, 0:1], 1.0 / DM, EPS, ALU.mult, ALU.add).then_inc(X["f_mean"], 1)

                def final_out(t):
                    dve.wait_ge(X["f_root"], t + 1)
                    vc.link(V.reciprocal(f_stat[:, 3:4], f_stat[:, 2:3]))
                    V.scalar_tensor_tensor(out_tile, h_now, f_stat[:, 3:4], gain_fin, ALU.mult, ALU.mult).then_inc(X["out_made"], 1)

                def step(t, j, first, last, jp, jn):
                    if at(j, START):
                        if not first:
                            dve.wait_ge(X["dot_made"], t * PICKS)
                        vc.link(V.tensor_copy(hf_now, hf_next))
                    for m in range(GROUPS):
                        for k in range(m * GROUP, (m + 1) * GROUP):
                            dve.wait_ge(got[k % RING], t * (PICKS * 16 // RING) + j * (TOPK * 16 // RING) + 16 * (k // RING + 1))
                            row = ring[k % RING][:, 0:DM]
                            V.tensor_tensor_reduce(out=row, in0=row, in1=hf_now, scale=1.0, scalar=0.0, op0=ALU.mult, op1=ALU.add,
                                                   accum_out=dots[:, k:k + 1]).then_inc(X["dot_made"], 1)
                        of = slice(m * GROUP, (m + 1) * GROUP)
                        made = t * (PHEADS * GROUPS) + j * GROUPS + (m + 1)
                        dve.wait_ge(X["gelu_made"], made)
                        V.scalar_tensor_tensor(weights[:, of], scored_gelu[:, of], gate_scale[:, ds(j, 1)],
                                               gates[:, ds(j * TOPK + m * GROUP, GROUP)], ALU.mult, ALU.mult).then_inc(X["weights_made"], 1)
                        if at(j, START) and not first:
                            if m == 0:
                                take_sum(t - 1)
                            if m == 1:
                                final_mean(t - 1)
                            if m == 2:
                                final_out(t - 1)
                        if m == 2 and at(j, START):
                            if not first:
                                dve.wait_ge(X["out_made"], t + 0)
                            move(t)
                        if at(j, TURN) and not last and m < 3:
                            (residual, next_mean, query)[m](t + 1)
                        if jp is not None:
                            pick(m, t, j, jp)
                        if m == 2 and jn is not None:
                            gate(t * PHEADS + (j + 1), jn)

                def tile(t, first=False, last=False):
                    step(t, START, first, last, AHEAD, 1)
                    V.sem_inc(vector_steps, 1)
                    with vc.loop(1, TURN, PICK_LINKS + 1) as j:
                        step(t, j, first, last, j + AHEAD, j + 1)
                    for j in range(TURN, PHEADS):
                        jp = None if last and j > TURN else (j + AHEAD) % PHEADS
                        jn = None if last and j == PHEADS - 1 else (j + 1) % PHEADS
                        step(t, j, first, last, jp, jn)

                PICK_LINKS = 18
                dve.wait_ge(gains_in, 32)
                V.memset(dots, 0.0).then_inc(X["used"], USED0)
                residual(0)
                next_mean(0)
                query(0)
                for n in range(AHEAD):
                    for piece in range(4):
                        pick(piece, 0, n - AHEAD, n)
                gate(0, 0)
                tile(0, first=True)
                with vc.loop(1, TILES - 1, PHEADS * (PICK_LINKS + 1) + 3) as t:
                    tile(t)
                tile(TILES - 1, last=True)
                take_sum(TILES - 1)
                final_mean(TILES - 1)
                final_out(TILES - 1)

            @block.tensor
            def _(pe):
                def turn(t):
                    pe.wait_ge(X["hf_made"], t + 1)
                    for d in range(DB):
                        m = PE.transpose(bank[d // 4][:, (d % 4) * P:(d % 4 + 1) * P], hf_next[:, d * P:(d + 1) * P], ident)
                    m.then_inc(X["hf_turned"], 1)

                def project(t, half):
                    if half == 0:
                        pe.wait_ge(X["mixed_in"], t * 16)
                        pe.wait_ge(X["h_made"], t + 0)
                    for d in range(DB):
                        m = PE.matmul(bank[3 + half], mixed[:, d * P:(d + 1) * P],
                                      w_out[:, d * DM + half * HALF:d * DM + (half + 1) * HALF], start=(d == 0), stop=(d == DB - 1))
                    if half == 1:
                        m.then_inc(mixed_out, 1)

                def head(n, j):
                    pe.wait_ge(X["picked"], n)
                    for d in range(DB):
                        m = PE.matmul(bank[2][:, 0:QD], hf_t[:, d * P:(d + 1) * P],
                                      w_score[:, ds(j * QD + d * (PHEADS * QD), QD)], start=(d == 0), stop=(d == DB - 1))
                    m.then_inc(X["scored"], 1)

                def step(t, j, first, after, jp):
                    if first:
                        pe.wait_ge(M["w_score_kept"], 2 * PHEADS if isinstance(j, int) and j > 0 else j * 2 + (2 * AHEAD + 2))
                    if jp is not None:
                        head(t * PHEADS + (j + AHEAD), jp)
                    if at(j, START) and not first:
                        pe.wait_ge(X["summed"], t + 0)
                    for k in range(TOPK):
                        pe.wait_ge(X["diag_made"], t * PICKS + j * TOPK + (k + 1))
                        for half in range(2):
                            m = PE.matmul(bank[6 + half], diag[k % RING], ring[k % RING][:, DM + half * HALF:DM + (half + 1) * HALF],
                                          start=(at(j, START) and k == 0), stop=(at(j, END) and k == TOPK - 1))
                        m.then_inc(X["used"], 1)
                        if k in (GROUP - 1, 3 * GROUP - 1) and makes_weights(first, j):
                            s = k // (2 * GROUP)
                            pe.wait_ge(some_in, j * 64 + 32 * (s + 1))
                            pe.wait_ge(M["w_score_kept"], j * 2 + (2 * HEADS_FIRST + s))
                            weight_product(some_queries, some_keys, bank[0:2])
                        if k == GROUP - 1 and after == 2 and isinstance(j, int) and j > TURN:
                            project(t + 2, j - TURN - 1)
                        if k == TOPK - 1 and at(j, TURN) and after:
                            turn(t + 1)

                def tile(t, first=False, after=2):
                    step(t, START, first, after, AHEAD)
                    with pe.Fori(1, TURN) as j:
                        step(t, j, first, after, j + AHEAD)
                    step(t, TURN, first, after, TURN + AHEAD)
                    if after:
                        pe.wait_ge(X["hf_kept"], t + 2)
                        pe.sem_inc(tensor_steps, 1)
                    for j in range(TURN + 1, PHEADS):
                        step(t, j, first, after, j + AHEAD - PHEADS if after else None)

                turn(0)
                pe.wait_ge(X["hf_kept"], 1)
                pe.sem_inc(tensor_steps, 1)
                head(0, 0)
                project(1, 0)
                project(1, 1)
                head(1, 1)
                tile(0, first=True)
                with pe.Fori(1, TILES - 2) as t:
                    tile(t)
                tile(TILES - 2, after=1)
                tile(TILES - 1, after=0)
    return nc


def kernel(x, norm_mix_gain, w_in, conv_w, a_log, dt_bias, gdn_out_gain, w_pool, b_pool, pool_scale, w_out,
           norm_ffn_gain, peer_w_query, peer_sub_keys_1, peer_sub_keys_2, peer_expert_u, peer_expert_v,
           norm_final_gain):
    import concourse.bacc as bacc
    from concourse.bass_utils import run_bass_kernel_spmd

    data = layout(x, norm_mix_gain, w_in, conv_w, a_log, dt_bias, gdn_out_gain, w_pool, b_pool, pool_scale, w_out,
                  norm_ffn_gain, peer_w_query, peer_sub_keys_1, peer_sub_keys_2, peer_expert_u, peer_expert_v,
                  norm_final_gain)
    nc = bacc.Bacc("TRN2", target_bir_lowering=False, num_devices=1)
    ins = {n: nc.dram_tensor("in_" + n, v.shape, mybir.dt.from_np(v.dtype), kind="ExternalInput").ap() for n, v in data.items()}
    out = nc.dram_tensor("out", (SEQ, DM), mybir.dt.float32, kind="ExternalOutput").ap()
    build(nc, ins, out)
    r = run_bass_kernel_spmd(nc, [{"in_" + n: v for n, v in data.items()}], core_ids=[0])
    return r.results[0]["out"].reshape(1, SEQ, DM)


def layout(x, norm_mix_gain, w_in, conv_w, a_log, dt_bias, gdn_out_gain, w_pool, b_pool, pool_scale, w_out,
           norm_ffn_gain, peer_w_query, peer_sub_keys_1, peer_sub_keys_2, peer_expert_u, peer_expert_v,
           norm_final_gain):
    def rows(w):
        w = np.asarray(w)
        return w.reshape(-1, P, w.shape[1]).transpose(1, 0, 2).reshape(P, -1)

    w_in = np.asarray(w_in)[0]
    n_mixed = HALF + 3 * HALF
    wc = w_in[:, :n_mixed].reshape(DB, P, n_mixed // P, P).transpose(2, 1, 0, 3).reshape(n_mixed // P, P, DM)
    taps = np.asarray(conv_w)[0].reshape(TAPS, 12, P).transpose(2, 1, 0).reshape(P, 12 * TAPS)
    keys = np.stack([np.asarray(peer_sub_keys_1)[0], np.asarray(peer_sub_keys_2)[0]], axis=1)
    data = {
        "x": np.asarray(x)[0],
        "constants": constants(),
        "gain_mix": np.asarray(norm_mix_gain)[0],
        "gain_ffn": np.asarray(norm_ffn_gain)[0],
        "gain_fin": np.asarray(norm_final_gain),
        "out_gain": np.asarray(gdn_out_gain)[0],
        "wc": wc,
        "wz": rows(w_in[:, n_mixed:n_mixed + HALF]),
        "wab": rows(w_in[:, n_mixed + HALF:]),
        "per_channel": np.concatenate([taps, np.asarray(b_pool)[0].T, np.asarray(pool_scale)[0].reshape(4, P).T], axis=1),
        "per_head": np.concatenate([np.asarray(a_log)[0], np.asarray(dt_bias)[0]]),
        "w_pool": np.asarray(w_pool)[0].transpose(1, 0, 2).reshape(P, 4 * P),
        "w_out": rows(np.asarray(w_out)[0]),
        "w_query": np.concatenate([np.asarray(peer_w_query)[0].reshape(DM, 2 * PHEADS, P).transpose(1, 2, 0),
                                   keys.reshape(2 * PHEADS, NKEYS, P).transpose(0, 2, 1)], axis=2),
        "experts": np.concatenate([np.asarray(peer_expert_u)[0], np.asarray(peer_expert_v)[0]], axis=1),
    }
    return {n: np.ascontiguousarray(v) for n, v in data.items()}
```
